# Optimizing a Trainium2 kernel written in Bass

```python
import math
import numpy as np
import jax
import jax.numpy as jnp
from jax import lax

D_MODEL = 1024
BATCH = 1
SEQ = 256
DEPTH = 1

SSD_WIDTH = D_MODEL
ATTN_WIDTH = D_MODEL
MIX_WIDTH = SSD_WIDTH + ATTN_WIDTH
SSD_HEAD_DIM = 64
SSD_HEADS = SSD_WIDTH // SSD_HEAD_DIM
SSD_GROUPS = 2
SSD_HEADS_PER_GROUP = SSD_HEADS // SSD_GROUPS
SSD_STATE = 128
SSD_CONV = 4
SSD_CHUNK = 128
SSD_CONV_DIM = SSD_WIDTH + 2 * SSD_GROUPS * SSD_STATE
ATTN_HEAD_DIM = 64
ATTN_HEADS = ATTN_WIDTH // ATTN_HEAD_DIM
KV_HEADS = 4
Q_PER_KV = ATTN_HEADS // KV_HEADS
KV_WIDTH = KV_HEADS * ATTN_HEAD_DIM
CMP_BLOCK = 32
CMP_STRIDE = 16
CMP_HIDDEN = 256
SLC_BLOCK = 64
SLC_TOPK = 16
WINDOW = 512
Q_BLOCK = 64
ROPE_THETA = 10000.0
N_GATES = 3
PEER_HEADS = 8
PEER_KEYS = 128
PEER_EXPERTS = PEER_KEYS * PEER_KEYS
PEER_KEY_DIM = 256
PEER_TOPK = 16
PEER_TOKEN_BLOCK = 128
DN_ALPHA = (2 * DEPTH) ** 0.25
DN_BETA = (8 * DEPTH) ** -0.25
LN_EPS = 1e-5
RMS_EPS = 1e-5
NEG_INF = -1e30
BIG = 1e30

SPLIT_SIZES = (SSD_WIDTH, SSD_CONV_DIM, SSD_HEADS, ATTN_WIDTH, 6 * KV_WIDTH, ATTN_HEADS * N_GATES)
IN_PROJ_DIM = sum(SPLIT_SIZES)
SPLIT_POINTS = tuple(int(v) for v in np.cumsum(SPLIT_SIZES)[:-1])

kernel_name = "hymba_ssd_nsa_peer_deepnorm"

def layer_norm(x, g, b):
    xf = x.astype(jnp.float32)
    mu = jnp.mean(xf, -1, keepdims=True)
    var = jnp.mean(jnp.square(xf - mu), -1, keepdims=True)
    return ((xf - mu) * lax.rsqrt(var + LN_EPS) * g + b).astype(x.dtype)

def rms_norm(x, g):
    xf = x.astype(jnp.float32)
    return xf * lax.rsqrt(jnp.mean(xf * xf, -1, keepdims=True) + RMS_EPS) * g

def rope_angles(pos):
    inv = ROPE_THETA ** (-jnp.arange(0, ATTN_HEAD_DIM, 2, dtype=jnp.float32) / ATTN_HEAD_DIM)
    ang = pos.astype(jnp.float32)[:, None] * inv[None, :]
    return jnp.cos(ang), jnp.sin(ang)

def apply_rope(x, cos, sin):
    x1, x2 = jnp.split(x.astype(jnp.float32), 2, axis=-1)
    c = cos[:, None, :]
    s = sin[:, None, :]
    return jnp.concatenate([x1 * c - x2 * s, x1 * s + x2 * c], -1).astype(x.dtype)

def causal_dwconv(x, w, b):
    y = lax.conv_general_dilated(
        x, w[:, None, :].astype(x.dtype), window_strides=(1,), padding=[(w.shape[0] - 1, 0)],
        dimension_numbers=("NWC", "WIO", "NWC"), feature_group_count=x.shape[-1])
    return y + b

def segsum(a):
    cs = jnp.cumsum(a, -1)
    T = a.shape[-1]
    diff = cs[..., :, None] - cs[..., None, :]
    return jnp.where(jnp.tril(jnp.ones((T, T), dtype=bool)), diff, -jnp.inf)

def ssd_chunked(xh, dt, A, Bm, Cm):
    b, L, G, K, P = xh.shape
    N = Bm.shape[-1]
    c, l = L // SSD_CHUNK, SSD_CHUNK
    xdt = (xh.astype(jnp.float32) * dt[..., None]).reshape(b, c, l, G, K, P)
    a = (dt * A).reshape(b, c, l, G, K).transpose(0, 3, 4, 1, 2)
    Bc = Bm.astype(jnp.float32).reshape(b, c, l, G, N)
    Cc = Cm.astype(jnp.float32).reshape(b, c, l, G, N)
    a_cs = jnp.cumsum(a, -1)
    Lmat = jnp.exp(segsum(a))
    CB = jnp.einsum('bclgn,bcsgn->bgcls', Cc, Bc)
    scores = CB[:, :, None] * Lmat
    y_diag = jnp.einsum('bgkcls,bcsgkp->bclgkp', scores, xdt)
    decay_states = jnp.exp(a_cs[..., -1:] - a_cs).transpose(0, 3, 4, 1, 2)
    states = jnp.einsum('bclgn,bclgkp->bcgkpn', Bc, xdt * decay_states[..., None])
    states = jnp.concatenate([jnp.zeros_like(states[:, :1]), states], axis=1)
    last = jnp.pad(a_cs[..., -1], ((0, 0), (0, 0), (0, 0), (1, 0)))
    chunk_decay = jnp.exp(segsum(last))
    new_states = jnp.einsum('bgkzc,bcgkpn->bzgkpn', chunk_decay, states)
    prev_states = new_states[:, :-1]
    out_decay = jnp.exp(a_cs).transpose(0, 3, 4, 1, 2)
    y_off = jnp.einsum('bclgn,bcgkpn->bclgkp', Cc, prev_states) * out_decay[..., None]
    return (y_diag + y_off).reshape(b, L, G, K, P)

def ssd_mixer(z, xbc, dt_raw, conv_w, conv_b, dt_bias, a_log, d_skip, norm_w):
    b, L, _ = z.shape
    xbc = jax.nn.silu(causal_dwconv(xbc, conv_w, conv_b))
    xs, Bm, Cm = jnp.split(xbc, [SSD_WIDTH, SSD_WIDTH + SSD_GROUPS * SSD_STATE], axis=-1)
    xh = xs.reshape(b, L, SSD_GROUPS, SSD_HEADS_PER_GROUP, SSD_HEAD_DIM)
    Bm = Bm.reshape(b, L, SSD_GROUPS, SSD_STATE)
    Cm = Cm.reshape(b, L, SSD_GROUPS, SSD_STATE)
    dt = jax.nn.softplus(dt_raw.astype(jnp.float32) + dt_bias.astype(jnp.float32))
    dt = dt.reshape(b, L, SSD_GROUPS, SSD_HEADS_PER_GROUP)
    A = -jnp.exp(a_log.astype(jnp.float32)).reshape(SSD_GROUPS, SSD_HEADS_PER_GROUP)
    y = ssd_chunked(xh, dt, A, Bm, Cm)
    y = y + d_skip.astype(jnp.float32).reshape(SSD_GROUPS, SSD_HEADS_PER_GROUP)[..., None] * xh.astype(jnp.float32)
    gw = SSD_HEADS_PER_GROUP * SSD_HEAD_DIM
    y = y.reshape(b, L, SSD_GROUPS, gw) * jax.nn.silu(z.astype(jnp.float32)).reshape(b, L, SSD_GROUPS, gw)
    y = rms_norm(y, norm_w.reshape(SSD_GROUPS, gw))
    return y.reshape(b, L, SSD_WIDTH)

def compress_blocks(k, cmp_idx, pos_emb, w1, w2):
    b, _, hk, dh = k.shape
    n = cmp_idx.shape[0]
    blocks = k[:, cmp_idx] + pos_emb[:, None, :]
    flat = blocks.transpose(0, 1, 3, 2, 4).reshape(b, n, hk, CMP_BLOCK * dh)
    return jax.nn.gelu(flat @ w1, approximate=False) @ w2

def nsa_mixer(q, k_cmp, v_cmp, k_slc, v_slc, k_win, v_win, gate_raw,
              cmp_pos_k, cmp_w1_k, cmp_w2_k, cmp_pos_v, cmp_w1_v, cmp_w2_v):
    b, L, _ = q.shape
    n_cmp = (L - CMP_BLOCK) // CMP_STRIDE + 1
    n_slc = L // SLC_BLOCK
    n_sel = min(SLC_TOPK, n_slc)
    n_qb = L // Q_BLOCK
    kv = lambda t: t.reshape(b, L, KV_HEADS, ATTN_HEAD_DIM)

    cos, sin = rope_angles(jnp.arange(L))
    qh = apply_rope(q.reshape(b, L, ATTN_HEADS, ATTN_HEAD_DIM), cos, sin) * (ATTN_HEAD_DIM ** -0.5)
    qh = qh.reshape(b, L, KV_HEADS, Q_PER_KV, ATTN_HEAD_DIM)
    gates = jax.nn.sigmoid(gate_raw.astype(jnp.float32)).reshape(b, L, KV_HEADS, Q_PER_KV, N_GATES)

    cmp_idx = np.arange(n_cmp)[:, None] * CMP_STRIDE + np.arange(CMP_BLOCK)[None, :]
    cmp_end_np = cmp_idx[:, -1]
    ccos, csin = rope_angles(jnp.asarray(cmp_end_np))
    kc = apply_rope(compress_blocks(kv(k_cmp), cmp_idx, cmp_pos_k, cmp_w1_k, cmp_w2_k), ccos, csin)
    vc = compress_blocks(kv(v_cmp), cmp_idx, cmp_pos_v, cmp_w1_v, cmp_w2_v)
    cmp_end = jnp.asarray(cmp_end_np)
    cs = np.arange(n_cmp) * CMP_STRIDE
    ss = np.arange(n_slc) * SLC_BLOCK
    overlap = jnp.asarray(((cs[:, None] < ss[None, :] + SLC_BLOCK) &
                           (cs[:, None] + CMP_BLOCK > ss[None, :])).astype(np.float32))

    ks = apply_rope(kv(k_slc), cos, sin)
    ks_blk = ks.reshape(b, n_slc, SLC_BLOCK, KV_HEADS, ATTN_HEAD_DIM).transpose(0, 3, 1, 2, 4)
    vs_blk = kv(v_slc).reshape(b, n_slc, SLC_BLOCK, KV_HEADS, ATTN_HEAD_DIM).transpose(0, 3, 1, 2, 4)
    gather_blocks = jax.vmap(jax.vmap(lambda kb, ii: kb[ii]))

    pad = ((0, 0), (WINDOW, 0), (0, 0), (0, 0))
    kw_pad = jnp.pad(apply_rope(kv(k_win), cos, sin), pad)
    vw_pad = jnp.pad(kv(v_win), pad)
    blk = jnp.arange(n_slc)

    def block(qi):
        start = qi * Q_BLOCK
        t = start + jnp.arange(Q_BLOCK)
        qb = lax.dynamic_slice_in_dim(qh, start, Q_BLOCK, axis=1)
        gb = lax.dynamic_slice_in_dim(gates, start, Q_BLOCK, axis=1)

        s_c = jnp.einsum('bqhgd,bnhd->bhgqn', qb, kc).astype(jnp.float32)
        valid_c = cmp_end[None, :] <= t[:, None]
        p_c = jnp.where(valid_c, jax.nn.softmax(jnp.where(valid_c, s_c, NEG_INF), -1), 0.0)
        o_c = jnp.einsum('bhgqn,bnhd->bqhgd', p_c, vc.astype(jnp.float32))

        imp = jnp.einsum('bhgqn,nj->bhqj', p_c, overlap)
        tb = t // SLC_BLOCK
        causal_b = blk[None, :] * SLC_BLOCK <= t[:, None]
        forced = (blk[None, :] == 0) | (blk[None, :] == tb[:, None]) | (blk[None, :] == tb[:, None] - 1)
        imp = jnp.where(causal_b, jnp.where(forced, BIG, imp), NEG_INF)
        top_s, top_i = lax.top_k(imp, n_sel)
        blk_ok = top_s > 0.5 * NEG_INF
        kg = gather_blocks(ks_blk, top_i)
        vg = gather_blocks(vs_blk, top_i)
        s_s = jnp.einsum('bqhgd,bhqjld->bhgqjl', qb, kg).astype(jnp.float32)
        key_pos = top_i[..., None] * SLC_BLOCK + jnp.arange(SLC_BLOCK)
        mask_s = blk_ok[..., None] & (key_pos <= t[None, None, :, None, None])
        s_s = jnp.where(mask_s[:, :, None], s_s, NEG_INF)
        sh = s_s.shape
        p_s = jax.nn.softmax(s_s.reshape(sh[:4] + (n_sel * SLC_BLOCK,)), -1).reshape(sh)
        o_s = jnp.einsum('bhgqjl,bhqjld->bqhgd', p_s, vg.astype(jnp.float32))

        kw_b = lax.dynamic_slice_in_dim(kw_pad, start, Q_BLOCK + WINDOW, axis=1)
        vw_b = lax.dynamic_slice_in_dim(vw_pad, start, Q_BLOCK + WINDOW, axis=1)
        kpos = start - WINDOW + jnp.arange(Q_BLOCK + WINDOW)
        mask_w = (kpos[None, :] <= t[:, None]) & (kpos[None, :] > t[:, None] - WINDOW) & (kpos[None, :] >= 0)
        s_w = jnp.einsum('bqhgd,bkhd->bhgqk', qb, kw_b).astype(jnp.float32)
        p_w = jax.nn.softmax(jnp.where(mask_w, s_w, NEG_INF), -1)
        o_w = jnp.einsum('bhgqk,bkhd->bqhgd', p_w, vw_b.astype(jnp.float32))

        return gb[..., 0:1] * o_c + gb[..., 1:2] * o_s + gb[..., 2:3] * o_w

    out = lax.map(block, jnp.arange(n_qb))
    return out.transpose(1, 0, 2, 3, 4, 5).reshape(b, L, ATTN_WIDTH)

def peer_ffn(x, w_query, sub_keys, expert_u, expert_v):
    b, L, D = x.shape
    T = b * L
    xt = x.reshape(T, D)
    q = (xt @ w_query).reshape(T, PEER_HEADS, 2, PEER_KEY_DIM // 2)
    s = jnp.einsum('thcd,hckd->thck', q, sub_keys).astype(jnp.float32)
    s_top, i_top = lax.top_k(s, PEER_TOPK)
    cand = (s_top[:, :, 0, :, None] + s_top[:, :, 1, None, :]).reshape(T, PEER_HEADS, PEER_TOPK * PEER_TOPK)
    cand_idx = (i_top[:, :, 0, :, None] * PEER_KEYS + i_top[:, :, 1, None, :]).reshape(T, PEER_HEADS, PEER_TOPK * PEER_TOPK)
    g_s, g_pos = lax.top_k(cand, PEER_TOPK)
    e_idx = jnp.take_along_axis(cand_idx, g_pos, axis=-1)
    g = jax.nn.softmax(g_s, -1)
    nb = T // PEER_TOKEN_BLOCK

    def block(args):
        xb, eb, gb = args
        u = expert_u[eb]
        h = jax.nn.gelu(jnp.einsum('td,thkd->thk', xb, u).astype(jnp.float32), approximate=False)
        v = expert_v[eb]
        return jnp.einsum('thk,thkd->td', (gb * h).astype(v.dtype), v)

    y = lax.map(block, (xt.reshape(nb, PEER_TOKEN_BLOCK, D),
                        e_idx.reshape(nb, PEER_TOKEN_BLOCK, PEER_HEADS, PEER_TOPK),
                        g.reshape(nb, PEER_TOKEN_BLOCK, PEER_HEADS, PEER_TOPK)))
    return y.reshape(b, L, D).astype(x.dtype)

def setup_inputs(seed: int = 0) -> dict:
    key = jax.random.key(seed)
    ks = jax.random.split(key, 24)
    f32 = jnp.float32
    nl = DEPTH

    def nrm(k, shape, scale):
        return jax.random.normal(k, shape, f32) * scale

    x = nrm(ks[0], (BATCH, SEQ, D_MODEL), 1.0)
    w_in = nrm(ks[1], (nl, D_MODEL, IN_PROJ_DIM), D_MODEL ** -0.5)
    conv_w = nrm(ks[2], (nl, SSD_CONV, SSD_CONV_DIM), SSD_CONV ** -0.5)
    conv_b = nrm(ks[3], (nl, SSD_CONV_DIM), 0.01)
    dt0 = jnp.exp(jax.random.uniform(ks[4], (nl, SSD_HEADS), f32, math.log(1e-3), math.log(1e-1)))
    dt_bias = dt0 + jnp.log(-jnp.expm1(-dt0))
    a_log = jnp.log(jax.random.uniform(ks[5], (nl, SSD_HEADS), f32, 1.0, 16.0))
    d_skip = 1.0 + nrm(ks[6], (nl, SSD_HEADS), 0.1)
    ssd_norm_w = 1.0 + nrm(ks[7], (nl, SSD_WIDTH), 0.02)
    cmp_in = CMP_BLOCK * ATTN_HEAD_DIM
    cmp_pos_k = nrm(ks[8], (nl, CMP_BLOCK, ATTN_HEAD_DIM), 0.02)
    cmp_w1_k = nrm(ks[9], (nl, cmp_in, CMP_HIDDEN), cmp_in ** -0.5)
    cmp_w2_k = nrm(ks[10], (nl, CMP_HIDDEN, ATTN_HEAD_DIM), CMP_HIDDEN ** -0.5)
    cmp_pos_v = nrm(ks[11], (nl, CMP_BLOCK, ATTN_HEAD_DIM), 0.02)
    cmp_w1_v = nrm(ks[12], (nl, cmp_in, CMP_HIDDEN), cmp_in ** -0.5)
    cmp_w2_v = nrm(ks[13], (nl, CMP_HIDDEN, ATTN_HEAD_DIM), CMP_HIDDEN ** -0.5)
    attn_norm_w = 1.0 + nrm(ks[14], (nl, ATTN_WIDTH), 0.02)
    w_out = nrm(ks[15], (nl, MIX_WIDTH, D_MODEL), (MIX_WIDTH ** -0.5) * DN_BETA)
    ln1_g = 1.0 + nrm(ks[16], (nl, D_MODEL), 0.02)
    ln1_b = nrm(ks[17], (nl, D_MODEL), 0.01)
    peer_w_query = nrm(ks[18], (nl, D_MODEL, PEER_HEADS * PEER_KEY_DIM), D_MODEL ** -0.5)
    peer_sub_keys = nrm(ks[19], (nl, PEER_HEADS, 2, PEER_KEYS, PEER_KEY_DIM // 2), (PEER_KEY_DIM // 2) ** -0.5)
    peer_u = nrm(ks[20], (nl, PEER_EXPERTS, D_MODEL), D_MODEL ** -0.5)
    peer_v = nrm(ks[21], (nl, PEER_EXPERTS, D_MODEL), DN_BETA)
    ln2_g = 1.0 + nrm(ks[22], (nl, D_MODEL), 0.02)
    ln2_b = nrm(ks[23], (nl, D_MODEL), 0.01)
    return {"x": x, "w_in": w_in, "conv_w": conv_w, "conv_b": conv_b, "dt_bias": dt_bias,
            "a_log": a_log, "d_skip": d_skip, "ssd_norm_w": ssd_norm_w,
            "cmp_pos_k": cmp_pos_k, "cmp_w1_k": cmp_w1_k, "cmp_w2_k": cmp_w2_k,
            "cmp_pos_v": cmp_pos_v, "cmp_w1_v": cmp_w1_v, "cmp_w2_v": cmp_w2_v,
            "attn_norm_w": attn_norm_w, "w_out": w_out, "ln1_g": ln1_g, "ln1_b": ln1_b,
            "peer_w_query": peer_w_query, "peer_sub_keys": peer_sub_keys,
            "peer_u": peer_u, "peer_v": peer_v, "ln2_g": ln2_g, "ln2_b": ln2_b}

def reference(x, w_in, conv_w, conv_b, dt_bias, a_log, d_skip, ssd_norm_w,
              cmp_pos_k, cmp_w1_k, cmp_w2_k, cmp_pos_v, cmp_w1_v, cmp_w2_v,
              attn_norm_w, w_out, ln1_g, ln1_b, peer_w_query, peer_sub_keys,
              peer_u, peer_v, ln2_g, ln2_b):
    h = x
    for i in range(DEPTH):
        proj = h @ w_in[i]
        z, xbc, dt_raw, q, kvs, gate_raw = jnp.split(proj, SPLIT_POINTS, axis=-1)
        k_cmp, v_cmp, k_slc, v_slc, k_win, v_win = jnp.split(kvs, 6, axis=-1)
        y_ssd = ssd_mixer(z, xbc, dt_raw, conv_w[i], conv_b[i], dt_bias[i], a_log[i], d_skip[i], ssd_norm_w[i])
        y_att = nsa_mixer(q, k_cmp, v_cmp, k_slc, v_slc, k_win, v_win, gate_raw,
                          cmp_pos_k[i], cmp_w1_k[i], cmp_w2_k[i], cmp_pos_v[i], cmp_w1_v[i], cmp_w2_v[i])
        y_att = rms_norm(y_att, attn_norm_w[i])
        mix = jnp.concatenate([y_ssd, y_att], axis=-1).astype(h.dtype) @ w_out[i]
        h = layer_norm(DN_ALPHA * h + mix, ln1_g[i], ln1_b[i])
        ffn = peer_ffn(h, peer_w_query[i], peer_sub_keys[i], peer_u[i], peer_v[i])
        h = layer_norm(DN_ALPHA * h + ffn, ln2_g[i], ln2_b[i])
    return h


_drawn_inputs = setup_inputs


def setup_inputs(seed=0):
    import zlib

    import numpy as np

    out = dict(_drawn_inputs(seed))
    spreads = {}
    factors = {'conv_b': 3.423,
     'cmp_pos_k': 6.22,
     'ln2_g': 22.575,
     'ln2_b': 46.531,
     'ssd_norm_w': 2.71,
     'attn_norm_w': 2.763}
    for name, (base, spread) in spreads.items():
        noise = np.random.default_rng([zlib.crc32(name.encode()), seed]).standard_normal(out[name].shape)
        drawn = base * np.exp(spread * noise) if base else spread * noise
        out[name] = jnp.asarray(drawn.astype(out[name].dtype))
    for name, factor in factors.items():
        out[name] = (out[name] * factor).astype(out[name].dtype)
    return out
```

```python
import math
from contextlib import ExitStack

import numpy as np
import concourse.bass as bass
from concourse import mybir

P = 128
D = 1024
T = 256
NT = T // P
KD = D // P
NH = 16
HD = 64
NG = 2
NKV = 4
GQ = NH // NKV
CONV_C = 1536
NCONV = CONV_C // P
TAPS = 4
NCMP = 15
CSTRIDE = 16
CLEN = 32
CHID = 256
SLOT = 32
PH = 8
NKEY = 128
TOPK = 16
NEXP = NKEY * NKEY
ALPHA = 2 ** 0.25
EPS = 1e-5
NEG = -1e30
BELOW = -3e38

Z0, XBC0, DT0, Q0, KC0, KS0, G0 = 0, 1024, 2560, 2576, 3600, 4112, 5136
W_IN = 5184
TM_PIECES = [(DT0, 347), (DT0 + 347, 347), (DT0 + 694, 346), (KS0, 358), (KS0 + 358, 357), (KS0 + 715, 357)]
TM_W = sum(n for _, n in TM_PIECES)
TM_Q = Q0 - DT0
TM_KV = KC0 - DT0
TM_G = TM_KV + G0 - KS0

C_ID, C_TRI, C_STRICT, C_MASK = 0, 128, 256, 384
C_ROPE = 512
C_CROPE = C_ROPE + NT * 4 * HD
C_CBIAS = C_CROPE + 2 * HD
C_CVALID = C_CBIAS + NT * NCMP
C_IOTA = C_CVALID + NT * NCMP
C_HEAD = C_IOTA + TOPK
C_ALL = C_HEAD + GQ

WSLOTS = 3
WPIECE = 4096
RING = 8
LAG = 3
DIAGS = 4
CHOOSE_STEPS = 23


def constants():
    c = np.zeros((P, C_ALL), np.float32)
    p, f = np.arange(P)[:, None], np.arange(P)[None, :]
    c[:, C_ID:C_ID + P] = p == f
    c[:, C_TRI:C_TRI + P] = p <= f
    c[:, C_STRICT:C_STRICT + P] = p > f
    c[:, C_MASK:C_MASK + P] = np.where(f <= p, 0, NEG)
    inv = np.float32(10000.0) ** (-np.arange(0, HD, 2, dtype=np.float32) / HD)

    def table(pos):
        a = pos.astype(np.float32)[:, None] * inv[None, :]
        cos, sin = np.cos(a), np.sin(a)
        return np.concatenate([cos, cos], 1), np.concatenate([-sin, sin], 1)

    for i in range(NT):
        cos, sin = table(np.arange(P) + i * P)
        at = C_ROPE + i * 4 * HD
        for j, v in enumerate((cos * HD ** -0.5, sin * HD ** -0.5, cos, sin)):
            c[:, at + j * HD:at + (j + 1) * HD] = v
        end = np.arange(NCMP) * CSTRIDE + CLEN - 1
        ok = end[None, :] <= (np.arange(P) + i * P)[:, None]
        c[:, C_CBIAS + i * NCMP:C_CBIAS + (i + 1) * NCMP] = np.where(ok, 0, NEG)
        c[:, C_CVALID + i * NCMP:C_CVALID + (i + 1) * NCMP] = ok
    cos, sin = table(np.arange(NCMP) * CSTRIDE + CLEN - 1)
    c[:NCMP, C_CROPE:C_CROPE + HD] = cos
    c[:NCMP, C_CROPE + HD:C_CROPE + 2 * HD] = sin
    c[:, C_IOTA:C_IOTA + TOPK] = np.arange(TOPK)[None, :]
    c[:, C_HEAD:C_HEAD + GQ] = (np.arange(P)[:, None] // SLOT) == np.arange(GQ)[None, :]
    return c


def units():
    return [(kv, gp, b) for kv in range(NKV) for gp in range(GQ // 2) for b in range(2)]


def bank_plan():
    jobs, turn = {}, [0] * 8

    def add(bank, *name):
        jobs[name] = (bank, turn[bank])
        turn[bank] += 1

    k = 0

    def rotate(*name):
        nonlocal k
        add(k % 6, *name)
        k += 1

    for c in range(NCONV):
        rotate("xbc", c)
    for c in range(4):
        rotate("cmp", c)
    for n in range(len(TM_PIECES)):
        for i in range(NT):
            rotate("tm", n, i)
    for n in range(2):
        for i in range(NT):
            rotate("z", n, i)
    for w in range(2):
        rotate("hid", w)
    for w in range(2):
        rotate("hidT", w)
    rotate("kc")
    rotate("vc")
    rotate("kcT")
    for i in range(NT):
        for half in range(2):
            rotate("xT", i, half)
    rotate("BT")
    rotate("acs")
    for i in range(NT):
        rotate("cb", i)
        for n in range(4):
            rotate("seg", i, n)
        for g in range(NG):
            rotate("yd", i, g)
        for g in range(NG):
            rotate("st" if i == 0 else "yo", g)
        for n in range(4):
            rotate("qT", i, n)
        for b in range(2):
            rotate("kT", i, b)
        rotate("sc", i)
        rotate("pcT", i)
        U = len(units())
        for u in range(-2, U):
            if u + 2 < U:
                add((u + 2) % 3, "S", i, u + 2)
            if u >= 0:
                add(3 + u % 2, "PT", i, u)
        k = 0
        for n in range(4):
            rotate("mT", i, n)
        for n in range(2):
            rotate("mix", i, n)
        for n in range(2):
            rotate("hT", i, n)
        for n in range(4):
            rotate("q", i, n)
        for n in range(4):
            rotate("qpT", i, n)
        for n in range(4):
            rotate("s", i, n)
    for i in range(NT):
        for n in range(2):
            add(2 * i + n, "y", i, n)
    return jobs


def layer(nc, x, xT, w_in, conv, prm, normw, posT, w1, w2, w_out, ln, wq, skT, uv, const, out):
    fp = mybir.dt.float32
    u32 = mybir.dt.uint32
    ALU = mybir.AluOpType
    ACT = mybir.ActivationFunctionType
    AX = mybir.AxisListType.X
    J = bank_plan()
    UN = units()

    ctx = ExitStack()
    with ctx:
        def sb(name, shape, dt=fp):
            return ctx.enter_context(nc.sbuf_tensor(name, shape, dt))

        def sem(name):
            return ctx.enter_context(nc.semaphore(name))

        cst = sb("cst", [P, C_ALL])
        wring = sb("wring", [P, WSLOTS * WPIECE])
        x_sb = sb("x_sb", [P, NT, D])
        h_sb = sb("h_sb", [P, NT, D])
        tm = sb("tm", [P, NT, TM_W])
        zs = sb("zs", [P, NT, D])
        xc = sb("xc", [P, NCONV, T])
        x_tm = sb("x_tm", [P, NT, D])
        S0 = sb("S0", [P, D])
        B_tm = sb("B_tm", [P, NG, P])
        sk = sb("sk", [P, 2 * PH, NKEY])
        s_all = sb("s_all", [P, (NT * PH + 1) * 2 * NKEY])
        lnw = sb("lnw", [P, 4, D])
        cw = sb("cw", [P, NCONV, TAPS + 1])
        pr = sb("pr", [P, 3, NH])
        nw = sb("nw", [P, 2 * KD])
        pos = sb("pos", [P, 2, CLEN // 2])
        w2s = sb("w2s", [P, 2, 2, HD])
        sg = sb("sg", [P, NT, 3 * NH])
        Vbd = sb("Vbd", [P, NKV, GQ, HD])
        kcT = sb("kcT", [HD, NKV, NCMP])
        kT = sb("kT", [HD, 2, NKV, T])
        CBm = sb("CBm", [P, NG, P])
        dtb = sb("dtb", [P, 8, NT, NH])
        a_sb = sb("a_sb", [P, NT, NH])
        ea = sb("ea", [P, NT, 2, NH])
        st = sb("st", [P, 64])
        bn = sb("bn", [P, 2, 6])
        bna = sb("bna", [P, 2])
        nmx = sb("nmx", [P, len(UN), 2])
        lsum = sb("lsum", [P, len(UN), 2])
        coef = sb("coef", [P, len(UN), 2])
        cst1 = sb("cst1", [P, 4, NH])

        tmp = sb("tmp", [P, 7664])

        def view(at, *shape, src=None, parts=P):
            size = math.prod(shape)
            v = (tmp if src is None else src)[0:parts, at:at + size]
            if len(shape) == 1:
                return v
            names = "abcd"[:len(shape)]
            kw = {n: s for n, s in zip(names[1:], shape[1:])}
            return v.rearrange(f"p ({' '.join(names)}) -> p {' '.join(names)}", **kw)

        xT_sb = view(0, KD, T)
        xbcT = view(2048, NCONV, T + TAPS - 1)
        kd = view(2048 + NCONV * (T + TAPS - 1), 2, NKV, T)
        flat = s_all
        Xc = view(0, 2, CLEN // 2, NKV * NCMP, src=flat)
        hg = view(1920, 2, CHID, src=flat, parts=NKV * NCMP)
        hTs = view(2432, 2, 2, NKV * NCMP, src=flat)
        hTr = view(2672, 2, NKV, GQ, SLOT, src=flat)
        kcr = view(3696, NKV, HD, src=flat, parts=NCMP)
        kcr2 = view(1920 + 2 * CHID - 512, NKV, HD, src=flat, parts=NCMP)
        Ma = view(0, NH, P)
        E = view(2048, NH, P)
        xdt = view(4096, D)
        xdd = view(5120, D)
        ymix = s_all[:, PH * 2 * NKEY:NT * PH * 2 * NKEY]
        qr = view(0, NH, HD)
        qt = view(1024, NH, HD)
        Pb = view(1024, 3, 2, T)
        qT = view(2560, NH, P, parts=HD)
        PTs = view(4608, 2, 2, NT, P)
        Pc = view(5632, NH, SLOT)
        Pe = view(6144, NH, NCMP)
        PcT = view(6384, NKV, P)
        kr = view(6896, NKV, HD)
        krt = view(7152, NKV, HD)
        kr2 = view(7408, NKV, HD)
        mixT = view(0, 2 * KD, P)
        qtok = view(0, 2 * PH * NKEY)
        qpT = view(2048, 2 * PH, P)
        r1 = view(4096, D)
        junk = view(5120, D)
        hT = view(6144, KD, P)
        ks = view(0, 2, NKEY)
        ks2 = view(256, 2, NKEY)
        cand = view(512, TOPK * TOPK)
        cand2 = view(768, TOPK * TOPK)
        hot = view(1024, 2 * TOPK * TOPK)
        hot2 = view(1536, 2 * TOPK * TOPK)
        dotj = view(2048, D)
        acc2 = view(3072, D)
        diag = view(4096, DIAGS, P)
        top = view(4608, 2, TOPK)
        topif = view(4640, 2, TOPK)
        gtop = view(4672, TOPK)
        pij = view(4688, 2, TOPK)
        eij = view(4720, 2, TOPK)
        gexp = view(4752, TOPK)
        gate = view(4768, 2, TOPK)
        gsm = view(4800, 4)
        hdot = view(4808, 2, TOPK)
        wact = view(4840, 2, 2, TOPK)
        zero = view(4912, P)
        outb = [view(5120, D), view(6144, D)]
        topi = sb("topi", [P, 2, TOPK], u32)
        gpos = sb("gpos", [P, 3, TOPK], u32)
        eidx = sb("eidx", [P, 2, TOPK], u32)

        ps = ctx.enter_context(nc.psum_tensor("ps", [P, 8, 512], fp))

        ident = cst[:, C_ID:C_ID + P]
        tri = cst[:, C_TRI:C_TRI + P]
        strict = cst[:, C_STRICT:C_STRICT + P]
        cmask = cst[:, C_MASK:C_MASK + P]

        full = [sem(f"bank{b}_full") for b in range(8)]
        free = [sem(f"bank{b}_free") for b in range(8)]
        w_here = [sem(f"w_here{s}") for s in range(WSLOTS)]
        c_here = sem("c_here")
        x_here = sem("x_here")
        xT_here = sem("xT_here")
        prm_here = sem("prm_here")
        sk_here = sem("sk_here")
        ln_here = sem("ln_here")
        dve_step = sem("dve_step")
        act_step = sem("act_step")
        pool_step = sem("pool_step")
        wout_used = sem("wout_used")
        pads_zero = sem("pads_zero")
        conv_done = sem("conv_done")
        silu_done = sem("silu_done")
        X_ready = [sem("Xk_ready"), sem("Xv_ready")]
        hTr_ready = sem("hTr_ready")
        hTr_zero = sem("hTr_zero")
        dt_in = sem("dt_in")
        dt_ln = sem("dt_ln")
        a_ready = sem("a_ready")
        Ma_ready = sem("Ma_ready")
        sco_ready = sem("sco_ready")
        xdt_ready = sem("xdt_ready")
        xdd_ready = sem("xdd_ready")
        y_ready = sem("y_ready")
        sq_ready = sem("sq_ready")
        ms_ready = sem("ms_ready")
        sd_ready = sem("sd_ready")
        qr_ready = sem("qr_ready")
        kr_ready = sem("kr_ready")
        kr_used = sem("kr_used")
        sg_ready = sem("sg_ready")
        cm_ready = sem("cm_ready")
        ce_ready = sem("ce_ready")
        pc_ready = sem("pc_ready")
        nm_ready = sem("nm_ready")
        p_ready = sem("p_ready")
        pv_done = sem("pv_done")
        o_taken = sem("o_taken")
        kcr_ready = sem("kcr_ready")
        pc_zero = sem("pc_zero")
        loop_step = sem("loop_step")
        dve_passed = sem("dve_passed")
        pool_passed = sem("pool_passed")
        ymix_ready = sem("ymix_ready")
        h_ready = sem("h_ready")
        scores_ready = sem("scores_ready")
        ks_ready = sem("ks_ready")
        ks_used = sem("ks_used")
        gs_ready = sem("gs_ready")
        ge_ready = sem("ge_ready")
        idx_ready = sem("idx_ready")
        gate_ready = sem("gate_ready")
        row_here = [sem(f"row_here{s}") for s in range(RING)]
        row_used = sem("row_used")
        dot_done = sem("dot_done")
        w_step = sem("w_step")
        diag_ready = sem("diag_ready")
        zero_ready = sem("zero_ready")
        out_ready = sem("out_ready")
        out_done = sem("out_done")

        def row(slot):
            at = slot * 2 * D
            if slot < 6:
                return wring[:, at:at + 2 * D]
            return tm[:, :, :].rearrange("p i n -> p (i n)")[:, (slot - 6) * 2 * D:(slot - 5) * 2 * D]

        def await_full(eng, *name):
            b, n = J[name]
            eng.wait_ge(full[b], n + 1)
            return ps[:, b, :]

        def await_free(eng, *name):
            b, n = J[name]
            if n:
                eng.wait_ge(free[b], n)
            return ps[:, b, :]

        def await_taken(eng, *name):
            b, n = J[name]
            eng.wait_ge(free[b], n + 1)

        def taken(ins, *name):
            ins.then_inc(free[J[name][0]], 1)

        def filled(ins, *name):
            ins.then_inc(full[J[name][0]], 1)

        def await_alone(eng, passed, what, value):
            eng.wait_ge(what, value)
            if not isinstance(value, int):
                eng.sem_inc(passed, 1)

        def bc(ap, axis, n):
            ap = ap.unsqueeze(axis)
            shape = list(ap.shape)
            shape[axis] = n
            return ap.to_broadcast(shape)

        def add_position(eng, w):
            half = CSTRIDE // 2
            for kv in range(NKV):
                for m in range(2):
                    pairs = kd[:, w, kv, m * CSTRIDE:(m + NCMP) * CSTRIDE].rearrange("p (n c j) -> p j c n", c=half, j=2)[:, 0, :, :]
                    rows = slice(m * half, (m + 1) * half)
                    last = eng.tensor_tensor(Xc[:, w, rows, kv * NCMP:(kv + 1) * NCMP], pairs, bc(pos[:, w, rows], 2, NCMP), ALU.add)
            return last

        pieces = []
        for n in range(3):
            pieces.append((w_in[:, XBC0 + 512 * n:XBC0 + 512 * (n + 1)], 512, ("xbc", 4 * n + 3)))
        pieces.append((w_in[:, KC0:KS0], 512, ("cmp", 3)))
        for n, (at, w) in enumerate(TM_PIECES):
            pieces.append((w_in[:, at:at + w], w, ("tm", n, NT - 1)))
        for n in range(2):
            pieces.append((w_in[:, Z0 + 512 * n:Z0 + 512 * (n + 1)], 512, ("z", n, NT - 1)))
        for w in range(2):
            pieces.append((w1[w], CHID, ("hid", w)))
        for i in range(NT):
            for n in range(4):
                pieces.append((w_out[512 * n:512 * (n + 1), :], D, 3 * i + n + 1 if n < 3 else ("mix", i, 1)))
            for n in range(4):
                pieces.append((wq[:, 512 * n:512 * (n + 1)], 512, ("q", i, n)))
        piece_no = iter(range(len(pieces)))

        def piece_view(k):
            src, n, _ = pieces[k]
            rows = src.shape[0] // P
            at = (k % WSLOTS) * WPIECE
            return wring[:, at:at + rows * n].rearrange("p (k n) -> p k n", k=rows)

        block = ctx.enter_context(nc.Block())

        @block.sync
        def _(sp):
            sp.dma_start(xT_sb, xT.rearrange("(k p) t -> p k t", p=P)).then_inc(xT_here, 16)
            for k, (src, n, _) in enumerate(pieces):
                if k == 2:
                    sp.dma_start(cst[:, :], const).then_inc(c_here, 16)
                    sp.dma_start(cw[:, :, :], conv).then_inc(prm_here, 16)
                    sp.dma_start(pr[:, :, :].rearrange("p a n -> p (a n)"), prm.to_broadcast([P, 3 * NH])).then_inc(prm_here, 16)
                    sp.dma_start(nw[:, :], normw).then_inc(prm_here, 16)
                    sp.dma_start(pos[:, :, :], posT).then_inc(prm_here, 16)
                    sp.dma_start(w2s[:, :, :, :].rearrange("p w c n -> p (w c) n"), w2.rearrange("w (c p) n -> p (w c) n", p=P)).then_inc(prm_here, 16)
                if k == 12:
                    sp.dma_start(x_sb[:, :, :], x.rearrange("(i p) n -> p i n", p=P)).then_inc(x_here, 16)
                    sp.dma_start(sk[:, :, :], skT).then_inc(sk_here, 16)
                    for j in range(4):
                        sp.dma_start(lnw[:, j, :], ln[j:j + 1, :].to_broadcast([P, D])).then_inc(ln_here, 16)
                if k >= WSLOTS:
                    end = pieces[k - WSLOTS][2]
                    if isinstance(end, int):
                        sp.wait_ge(wout_used, end)
                    else:
                        await_full(sp, *end)
                sp.dma_start(piece_view(k), src.rearrange("(k p) n -> p k n", p=P)).then_inc(w_here[k % WSLOTS], 16)
            for i in range(NT):
                sp.wait_ge(out_ready, i + 1)
                sp.dma_start(out[i * P:(i + 1) * P, :], outb[i]).then_inc(out_done, 16)
            sp.wait_ge(out_done, 16 * NT)

        @block.tensor
        def _(pe):
            mm = nc.tensor.matmul
            tr = nc.tensor.transpose

            def next_piece():
                k = next(piece_no)
                pe.wait_ge(w_here[k % WSLOTS], 16 * (k // WSLOTS + 1))
                return piece_view(k)

            pe.wait_ge(xT_here, 16)
            for kind, count in (("xbc", NCONV), ("cmp", 4)):
                for c in range(count):
                    if c % 4 == 0:
                        w = next_piece()
                    o = await_free(pe, kind, c)
                    for k in range(KD):
                        last = mm(o[:, 0:T], w[:, k, (c % 4) * P:(c % 4 + 1) * P], xT_sb[:, k, :], start=k == 0, stop=k == KD - 1)
                    filled(last, kind, c)
            for kind, widths in (("tm", [n for _, n in TM_PIECES]), ("z", [512, 512])):
                for n, width in enumerate(widths):
                    w = next_piece()
                    for i in range(NT):
                        o = await_free(pe, kind, n, i)
                        for k in range(KD):
                            last = mm(o[:, 0:width], xT_sb[:, k, i * P:(i + 1) * P], w[:, k, :], start=k == 0, stop=k == KD - 1)
                        filled(last, kind, n, i)

            pe.wait_ge(c_here, 16)
            for w in range(2):
                wt = next_piece()
                pe.wait_ge(X_ready[w], 1)
                o = await_free(pe, "hid", w)
                for c in range(CLEN // 2):
                    last = mm(o[0:NKV * NCMP, 0:CHID], Xc[:, w, c, :], wt[:, c, :], start=c == 0, stop=c == CLEN // 2 - 1)
                filled(last, "hid", w)
            for w in range(2):
                await_taken(pe, "hid", w)
                o = await_free(pe, "hidT", w)
                for c in range(2):
                    last = tr(o[:, c * NKV * NCMP:(c + 1) * NKV * NCMP], hg[:, w, c * P:(c + 1) * P], ident[0:NKV * NCMP, 0:NKV * NCMP])
                filled(last, "hidT", w)
            await_taken(pe, "hidT", 0)
            pe.wait_ge(prm_here, 80)
            o = await_free(pe, "kc")
            for kv in range(NKV):
                for c in range(2):
                    last = mm(o[0:NCMP, kv * HD:(kv + 1) * HD], hTs[:, 0, c, kv * NCMP:(kv + 1) * NCMP], w2s[:, 0, c, :], start=c == 0, stop=c == 1)
            filled(last, "kc")
            pe.wait_ge(hTr_ready, 1)
            o = await_free(pe, "vc")
            for kv in range(NKV):
                for c in range(2):
                    last = mm(o[:, kv * HD:(kv + 1) * HD], hTr[:, c, kv, :, :].rearrange("p g n -> p (g n)"), w2s[:, 1, c, :], start=c == 0, stop=c == 1)
            filled(last, "vc")
            pe.wait_ge(kcr_ready, 1)
            o = await_free(pe, "kcT")
            for kv in range(NKV):
                last = tr(o[0:HD, kv * NCMP:(kv + 1) * NCMP], kcr[:, kv, :], ident[0:NCMP, 0:NCMP])
            filled(last, "kcT")

            pe.wait_ge(silu_done, 3)
            for i in range(NT):
                for half in range(2):
                    o = await_free(pe, "xT", i, half)
                    for c in range(4):
                        last = tr(o[:, c * P:(c + 1) * P], xc[:, 4 * half + c, i * P:(i + 1) * P], ident)
                    filled(last, "xT", i, half)
            o = await_free(pe, "BT")
            for g in range(NG):
                last = tr(o[:, g * P:(g + 1) * P], xc[:, KD + g, 0:P], ident)
            filled(last, "BT")
            pe.wait_ge(a_ready, 1)
            o = await_free(pe, "acs")
            for i in range(NT):
                for n, m in enumerate((tri, strict)):
                    at = (2 * i + n) * NH
                    last = mm(o[:, at:at + NH], m, a_sb[:, i, :], start=True, stop=True)
            filled(last, "acs")

            for i in range(NT):
                cols = slice(i * P, (i + 1) * P)
                o = await_free(pe, "cb", i)
                for g in range(NG):
                    last = mm(o[:, g * P:(g + 1) * P], xc[:, KD + g, cols], xc[:, KD + NG + g, cols], start=True, stop=True)
                filled(last, "cb", i)
                pe.wait_ge(Ma_ready, i + 1)
                for n in range(4):
                    o = await_free(pe, "seg", i, n)
                    filled(mm(o, strict, Ma[:, 4 * n:4 * n + 4, :].rearrange("p h l -> p (h l)"), start=True, stop=True), "seg", i, n)
                pe.wait_ge(xdt_ready, i + 1)
                for g in range(NG):
                    o = await_free(pe, "yd", i, g)
                    for k in range(NH // NG):
                        h = g * NH // NG + k
                        if k % 4 == 0:
                            pe.wait_ge(sco_ready, 4 * i + h // 4 + 1)
                        last = mm(o[:, k * HD:(k + 1) * HD], E[:, h, :], xdt[:, h * HD:(h + 1) * HD], start=True, stop=True)
                    filled(last, "yd", i, g)
                if i == 0:
                    pe.wait_ge(xdd_ready, 1)
                    await_taken(pe, "BT")
                    for g in range(NG):
                        o = await_free(pe, "st", g)
                        filled(mm(o, B_tm[:, g, :], xdd[:, g * 512:(g + 1) * 512], start=True, stop=True), "st", g)
                else:
                    for g in range(NG):
                        await_taken(pe, "st", g)
                        o = await_free(pe, "yo", g)
                        filled(mm(o, xc[:, KD + NG + g, cols], S0[:, g * 512:(g + 1) * 512], start=True, stop=True), "yo", g)

                pe.wait_ge(qr_ready, i + 1)
                for n in range(4):
                    o = await_free(pe, "qT", i, n)
                    for g in range(4):
                        last = tr(o[0:HD, g * P:(g + 1) * P], qr[:, 4 * n + g, :], ident)
                    filled(last, "qT", i, n)
                for b in range(2):
                    pe.wait_ge(kr_ready, 2 * i + b + 1)
                    o = await_free(pe, "kT", i, b)
                    src = kr if b == 0 else kr2
                    for kv in range(NKV):
                        last = tr(o[0:HD, kv * P:(kv + 1) * P], src[:, kv, :], ident)
                    filled(last, "kT", i, b)
                for n in range(4):
                    await_taken(pe, "qT", i, n)
                if i == 0:
                    await_taken(pe, "kcT")
                o = await_free(pe, "sc", i)
                for h in range(NH):
                    last = mm(o[:, h * NCMP:(h + 1) * NCMP], qT[:, h, :], kcT[:, h // GQ, :], start=True, stop=True)
                filled(last, "sc", i)
                pe.wait_ge(pc_ready, i + 1)
                o = await_free(pe, "pcT", i)
                for kv in range(NKV):
                    last = tr(o[:, kv * P:(kv + 1) * P], Pc[:, kv * GQ:(kv + 1) * GQ, :].rearrange("p g n -> p (g n)"), ident)
                filled(last, "pcT", i)
                for b in range(2):
                    await_taken(pe, "kT", i, b)

                def scores(u):
                    kv, gp, b = UN[u]
                    o = await_free(pe, "S", i, u)
                    for e in range(2):
                        h = kv * GQ + 2 * gp + e
                        n = (i + 1) * P
                        mm(o[:, e * T:e * T + n], qT[:, h, :], kT[:, b, kv, 0:n], start=True, stop=False, skip_group_check=True)
                        last = mm(o[:, e * T + i * P:e * T + n], ident, cmask, start=False, stop=True, skip_group_check=True)
                    filled(last, "S", i, u)

                def values(u):
                    kv, gp, b = UN[u]
                    await_taken(pe, "PT", i, u)
                    for e in range(2):
                        h = kv * GQ + 2 * gp + e
                        o = ps[:, 6 + h // 8, (h % 8) * HD:(h % 8 + 1) * HD]
                        for j in range(i + 1):
                            v = tm[:, j, TM_KV + 256 + 512 * b + kv * HD:TM_KV + 256 + 512 * b + (kv + 1) * HD]
                            last = mm(o, PTs[:, u % 2, e, j, :], v, start=False, stop=b == 1 and j == i, skip_group_check=True)
                    last.then_inc(pv_done, 1)

                if i:
                    pe.wait_ge(o_taken, 2 * i)
                else:
                    await_taken(pe, "vc")
                await_taken(pe, "pcT", i)
                for u in range(-2, len(UN) + 1):
                    if 0 <= u + 2 < len(UN):
                        scores(u + 2)
                    if 0 <= u < len(UN):
                        pe.wait_ge(p_ready, len(UN) * i + u + 1)
                        o = await_free(pe, "PT", i, u)
                        for e in range(2):
                            for j in range(i + 1):
                                last = tr(o[:, (2 * e + j) * P:(2 * e + j + 1) * P], Pb[:, u % 3, e, j * P:(j + 1) * P], ident)
                        filled(last, "PT", i, u)
                    if u >= 1:
                        if (u - 1) % 4 == 0:
                            kv = (u - 1) // 4
                            mm(ps[:, 6 + kv // 2, (kv % 2) * GQ * HD:(kv % 2 + 1) * GQ * HD], PcT[:, kv, :],
                               Vbd[:, kv, :, :].rearrange("p g n -> p (g n)"), start=True, stop=False, skip_group_check=True)
                        values(u - 1)

                pe.wait_ge(ymix_ready, i + 1)
                for n in range(4):
                    o = await_free(pe, "mT", i, n)
                    for c in range(4):
                        last = tr(o[:, c * P:(c + 1) * P], ymix[:, (4 * n + c) * P:(4 * n + c + 1) * P], ident)
                    filled(last, "mT", i, n)
                o = [await_free(pe, "mix", i, half) for half in range(2)]
                for n in range(4):
                    w = next_piece()
                    await_taken(pe, "mT", i, n)
                    for c in range(4):
                        for half in range(2):
                            last = mm(o[half], mixT[:, 4 * n + c, :], w[:, c, half * 512:(half + 1) * 512], start=n + c == 0, stop=n + c == 6)
                            if n + c == 6:
                                filled(last, "mix", i, half)
                    if n < 3:
                        last.then_inc(wout_used, 1)
                pe.wait_ge(h_ready, i + 1)
                for n in range(2):
                    o = await_free(pe, "hT", i, n)
                    for c in range(4):
                        last = tr(o[:, c * P:(c + 1) * P], h_sb[:, i, (4 * n + c) * P:(4 * n + c + 1) * P], ident)
                    filled(last, "hT", i, n)
                for n in range(2):
                    await_taken(pe, "hT", i, n)
                for n in range(4):
                    w = next_piece()
                    o = await_free(pe, "q", i, n)
                    for k in range(KD):
                        last = mm(o, hT[:, k, :], w[:, k, :], start=k == 0, stop=k == KD - 1)
                    filled(last, "q", i, n)
                for n in range(4):
                    await_taken(pe, "q", i, n)
                    o = await_free(pe, "qpT", i, n)
                    for c in range(4):
                        last = tr(o[:, c * P:(c + 1) * P], qtok[:, (4 * n + c) * P:(4 * n + c + 1) * P], ident)
                    filled(last, "qpT", i, n)
                pe.wait_ge(sk_here, 16)
                for n in range(4):
                    await_taken(pe, "qpT", i, n)
                    o = await_free(pe, "s", i, n)
                    for c in range(4):
                        last = mm(o[:, c * NKEY:(c + 1) * NKEY], qpT[:, 4 * n + c, :], sk[:, 4 * n + c, :], start=True, stop=True)
                    filled(last, "s", i, n)

            for i in range(NT):
                pe.wait_ge(zero_ready, 1)
                o = [await_free(pe, "y", i, n) for n in range(2)]
                for n in range(2):
                    mm(o[n], zero, sk[:, 0:4, :].rearrange("p a b -> p (a b)"), start=True, stop=False, skip_group_check=True)
                with pe.Fori(0, PH // 2) as pair:
                    for e in range(2):
                        for k in range(TOPK):
                            step = e * TOPK + k
                            pe.wait_ge(diag_ready, pair * (2 * TOPK) + (PH * i * TOPK + step + 1))
                            v_row = row(step % RING)[:, D:2 * D]
                            for n in range(2):
                                last = mm(o[n], diag[:, step % DIAGS, :], v_row[:, n * 512:(n + 1) * 512], start=False, stop=False, skip_group_check=True)
                            last.then_inc(row_used, 1)
                for n in range(2):
                    filled(mm(o[n], zero, sk[:, 0:4, :].rearrange("p a b -> p (a b)"), start=False, stop=True, skip_group_check=True), "y", i, n)

        @block.scalar
        def _(act):
            steps = [0]

            def f(out, in_, func, **kw):
                return nc.scalar.activation(out, in_, func, **kw)

            def link(ins):
                steps[0] += 1
                ins.then_inc(act_step, 1)
                act.wait_ge(act_step, steps[0])

            act.wait_ge(pads_zero, 1)
            for c in range(NCONV):
                o = await_full(act, "xbc", c)
                taken(f(xbcT[:, c, TAPS - 1:], o[:, 0:T], ACT.Copy), "xbc", c)
            for c in range(4):
                o = await_full(act, "cmp", c)
                w, kv = c // 2, 2 * (c % 2)
                for e in range(2):
                    rows = slice(e * HD, (e + 1) * HD)
                    f(kd[0:HD, w, kv + e, :], o[rows, 0:T], ACT.Copy)
                    last = f(kd[HD:P, w, kv + e, 0:T - 1], o[rows, 1:T], ACT.Copy)
                taken(last, "cmp", c)
            at = 0
            for n, (_, width) in enumerate(TM_PIECES):
                for i in range(NT):
                    o = await_full(act, "tm", n, i)
                    taken(f(tm[:, i, at:at + width], o[:, 0:width], ACT.Copy), "tm", n, i)
                at += width
            for n in range(2):
                for i in range(NT):
                    o = await_full(act, "z", n, i)
                    taken(f(zs[:, i, n * 512:(n + 1) * 512], o, ACT.Silu), "z", n, i)
            for n in range(3):
                act.wait_ge(conv_done, 4 * (n + 1))
                f(xc[:, 4 * n:4 * n + 4, :], xc[:, 4 * n:4 * n + 4, :], ACT.Silu).then_inc(silu_done, 1)
            for w in range(2):
                o = await_full(act, "hid", w)
                taken(f(hg[:, w, :], o[0:NKV * NCMP, 0:CHID], ACT.Gelu), "hid", w)
            for w in range(2):
                o = await_full(act, "hidT", w)
                taken(f(hTs[:, w, :, :], o[:, 0:2 * NKV * NCMP].rearrange("p (c n) -> p c n", c=2), ACT.Copy), "hidT", w)
            act.wait_ge(dt_in, 1)
            link(f(dtb[:, 2, :, :], dtb[:, 1, :, :], ACT.Exp))
            f(dtb[:, 7, 0, :], pr[:, 1, :], ACT.Exp)
            f(dtb[:, 3, :, :], dtb[:, 2, :, :], ACT.Ln, bias=1.0).then_inc(dt_ln, 1)
            o = await_full(act, "kcT")
            taken(f(kcT[:, :, :], o[0:HD, 0:NKV * NCMP].rearrange("p (k n) -> p k n", k=NKV), ACT.Copy), "kcT")
            for i in range(NT):
                for half in range(2):
                    o = await_full(act, "xT", i, half)
                    taken(f(x_tm[:, i, half * 512:(half + 1) * 512], o, ACT.Copy), "xT", i, half)
            o = await_full(act, "BT")
            taken(f(B_tm[:, :, :], o[:, 0:NG * P].rearrange("p (g n) -> p g n", g=NG), ACT.Copy), "BT")
            o = await_full(act, "acs")
            taken(f(ea[:, :, :, :], o[:, 0:NT * 2 * NH].rearrange("p (i n h) -> p i n h", i=NT, n=2), ACT.Exp), "acs")
            f(sg[:, :, :], tm[:, :, TM_G:TM_G + 3 * NH], ACT.Sigmoid).then_inc(sg_ready, 1)

            def rms_sum(src, n, width, at, value):
                for g in range(n):
                    last = f(xdd[:, g * width:(g + 1) * width], src[:, g * width:(g + 1) * width], ACT.Square, accum_out=st[:, at + g:at + g + 1])
                last.then_inc(sq_ready, 1)

            def root(at, n, value):
                act.wait_ge(ms_ready, value)
                f(st[:, at + 8:at + 8 + n], st[:, at + 4:at + 4 + n], ACT.Sqrt).then_inc(sd_ready, 1)

            for i in range(NT):
                for n in range(4):
                    o = await_full(act, "seg", i, n)
                    taken(f(E[:, 4 * n:4 * n + 4, :], o.rearrange("p (h l) -> p h l", h=4), ACT.Exp), "seg", i, n)
                if i == 0:
                    for g in range(NG):
                        o = await_full(act, "st", g)
                        taken(f(S0[:, g * 512:(g + 1) * 512], o, ACT.Copy), "st", g)
                act.wait_ge(y_ready, i + 1)
                rms_sum(ymix, NG, 512, 0, i)
                root(0, NG, 3 * i + 1)
                for n in range(4):
                    o = await_full(act, "qT", i, n)
                    taken(f(qT[:, 4 * n:4 * n + 4, :], o[0:HD, :].rearrange("p (h t) -> p h t", h=4), ACT.Copy), "qT", i, n)
                for b in range(2):
                    o = await_full(act, "kT", i, b)
                    taken(f(kT[:, b, :, i * P:(i + 1) * P], o[0:HD, :].rearrange("p (h t) -> p h t", h=NKV), ACT.Copy), "kT", i, b)
                act.wait_ge(cm_ready, i + 1)
                f(Pe, Pe, ACT.Exp).then_inc(ce_ready, 1)
                o = await_full(act, "pcT", i)
                taken(f(PcT, o.rearrange("p (h t) -> p h t", h=NKV), ACT.Copy), "pcT", i)

                def exps(u):
                    n = (i + 1) * P
                    act.wait_ge(nm_ready, len(UN) * i + u + 1)
                    o = await_full(act, "S", i, u)
                    if u >= 3:
                        await_full(act, "PT", i, u - 3)
                    for e in range(2):
                        last = f(Pb[:, u % 3, e, 0:n], o[:, e * T:e * T + n], ACT.Exp, bias=nmx[:, u, e:e + 1], accum_out=lsum[:, u, e:e + 1])
                    taken(last, "S", i, u)

                for u in range(-2, len(UN)):
                    if u + 2 < len(UN):
                        exps(u + 2)
                    if u >= 0:
                        o = await_full(act, "PT", i, u)
                        if u >= 2:
                            act.wait_ge(pv_done, len(UN) * i + u - 1)
                        taken(f(PTs[:, u % 2, :, 0:i + 1, :], o.rearrange("p (e j t) -> p e j t", e=2, j=NT)[:, :, 0:i + 1, :], ACT.Copy), "PT", i, u)
                act.wait_ge(o_taken, 2 * (i + 1))
                rms_sum(ymix[:, D:2 * D], 1, D, 12, i)
                root(12, 1, 3 * i + 2)
                root(24, 1, 3 * i + 3)
                for n in range(2):
                    o = await_full(act, "hT", i, n)
                    taken(f(hT[:, 4 * n:4 * n + 4, :], o.rearrange("p (h t) -> p h t", h=4), ACT.Copy), "hT", i, n)
                for n in range(4):
                    o = await_full(act, "q", i, n)
                    taken(f(qtok[:, n * 512:(n + 1) * 512], o, ACT.Copy), "q", i, n)
                for n in range(4):
                    o = await_full(act, "s", i, n)
                    at = i * PH * 2 * NKEY + n * 512
                    taken(f(s_all[:, at:at + 512], o, ACT.Copy), "s", i, n)

            def head_scores(u):
                act.wait_ge(ks_used, u + 1)
                nc.scalar.copy(ks.rearrange("p c n -> p (c n)"), s_all[:, bass.ds(u * (2 * NKEY), 2 * NKEY)]).then_inc(ks_ready, 1)

            def soft(u):
                act.wait_ge(gs_ready, u + 1)
                f(gexp, gtop, ACT.Exp, bias=gsm[:, 0:1], accum_out=gsm[:, 1:2]).then_inc(ge_ready, 1)

            act.wait_ge(zero_ready, 1)
            head_scores(0)
            soft(0)
            for i in range(NT):
                with act.Fori(0, PH // 2) as pair:
                    for e in range(2):
                        u = pair * 2 + (i * PH + e)
                        head_scores(u + 1)
                        for k in range(TOPK):
                            act.wait_ge(dot_done, u * TOPK + (k + 1))
                            f(wact[:, e, 0, k:k + 1], hdot[:, e, k:k + 1], ACT.Gelu).then_inc(w_step, 1)
                            if k == TOPK // 2 - 1:
                                soft(u + 1)
                root(36, 1, 3 * NT + i + 1)

        @block.vector
        def _(dve):
            V = nc.vector
            steps = [0]

            def link(ins):
                steps[0] += 1
                ins.then_inc(dve_step, 1)
                dve.wait_ge(dve_step, steps[0])

            def tt(out, a, b, op):
                return V.tensor_tensor(out, a, b, op)

            dve.wait_ge(prm_here, 80)
            for c in range(NCONV):
                await_taken(dve, "xbc", c)
                link(V.tensor_scalar(xc[:, c, :], xbcT[:, c, 0:T], cw[:, c, 0:1], cw[:, c, TAPS:TAPS + 1], ALU.mult, ALU.add))
                for k in range(1, TAPS):
                    ins = V.scalar_tensor_tensor(xc[:, c, :], xbcT[:, c, k:k + T], cw[:, c, k:k + 1], xc[:, c, :], ALU.mult, ALU.add)
                    if k < TAPS - 1:
                        link(ins)
                    else:
                        ins.then_inc(conv_done, 1)
            for c in range(2):
                await_taken(dve, "cmp", c)
            add_position(V, 0).then_inc(X_ready[0], 1)
            for i in range(NT):
                await_taken(dve, "tm", 0, i)
            link(tt(dtb[:, 0, :, :], tm[:, :, 0:NH], bc(pr[:, 0, :], 1, NT), ALU.add))
            V.scalar_tensor_tensor(dtb[:, 1, :, :], dtb[:, 0, :, :], -1.0, dtb[:, 0, :, :], ALU.mult, ALU.min).then_inc(dt_in, 1)
            V.tensor_scalar(dtb[:, 6, :, :], dtb[:, 0, :, :], 0.0, None, ALU.max)
            dve.wait_ge(dt_ln, 1)
            link(V.tensor_scalar(dtb[:, 4, :, :], dtb[:, 2, :, :], 1.0, None, ALU.add))
            link(V.tensor_scalar(dtb[:, 5, :, :], dtb[:, 4, :, :], -1.0, None, ALU.add))
            link(tt(dtb[:, 5, :, :], dtb[:, 2, :, :], dtb[:, 5, :, :], ALU.subtract))
            link(V.reciprocal(dtb[:, 4, :, :], dtb[:, 4, :, :]))
            link(tt(dtb[:, 5, :, :], dtb[:, 5, :, :], dtb[:, 4, :, :], ALU.mult))
            link(tt(dtb[:, 5, :, :], dtb[:, 5, :, :], dtb[:, 3, :, :], ALU.add))
            link(tt(dtb[:, 5, :, :], dtb[:, 5, :, :], dtb[:, 6, :, :], ALU.add))
            V.scalar_tensor_tensor(a_sb[:, :, :], dtb[:, 5, :, :], -1.0, bc(dtb[:, 7, 0, :], 1, NT), ALU.mult, ALU.mult).then_inc(a_ready, 1)
            dt = dtb[:, 5, :, :]
            dve.wait_ge(c_here, 16)
            await_taken(dve, "hidT", 1)
            dve.wait_ge(hTr_zero, 1)
            for g in range(GQ):
                last = V.tensor_copy(hTr[:, :, :, g, 0:NCMP], hTs[:, 1, :, :].rearrange("p c (k n) -> p c k n", k=NKV))
            last.then_inc(hTr_ready, 1)
            o = await_full(dve, "kc")[0:NCMP, 0:NKV * HD].rearrange("p (k d) -> p k d", k=NKV)
            cr = cst[0:NCMP, C_CROPE:C_CROPE + 2 * HD]
            link(tt(kcr, o, bc(cr[:, 0:HD], 1, NKV), ALU.mult))
            tt(kcr2[:, :, 0:HD // 2], o[:, :, HD // 2:HD], bc(cr[:, HD:HD + HD // 2], 1, NKV), ALU.mult)
            taken(tt(kcr2[:, :, HD // 2:HD], o[:, :, 0:HD // 2], bc(cr[:, HD + HD // 2:2 * HD], 1, NKV), ALU.mult), "kc")
            await_taken(dve, "kc")
            tt(kcr, kcr, kcr2, ALU.add).then_inc(kcr_ready, 1)
            o = await_full(dve, "vc")
            for kv in range(NKV):
                last = tt(Vbd[:, kv, :, :], bc(o[:, kv * HD:(kv + 1) * HD], 1, GQ), bc(cst[:, C_HEAD:C_HEAD + GQ], 2, HD), ALU.mult)
            taken(last, "vc")

            def rms(at, n, width, nth, value):
                dve.wait_ge(sq_ready, nth)
                V.tensor_scalar(st[:, at + 4:at + 4 + n], st[:, at:at + n], 1.0 / width, EPS, ALU.mult, ALU.add).then_inc(ms_ready, 1)
                dve.wait_ge(sd_ready, value)
                link(V.reciprocal(st[:, at:at + n], st[:, at + 8:at + 8 + n]))

            def layer_norm(dst, src, scratch, which, at, value):
                for n in range(2):
                    last = V.bn_stats(bn[:, n, :], src[:, n * 512:(n + 1) * 512])
                link(last)
                link(V.bn_aggr(bna[:, :], bn[:, :, :]))
                V.tensor_scalar(st[:, at + 4:at + 5], bna[:, 1:2], EPS, None, ALU.add).then_inc(ms_ready, 1)
                dve.wait_ge(sd_ready, value)
                link(V.reciprocal(st[:, at:at + 1], st[:, at + 8:at + 9]))
                link(V.tensor_scalar(scratch, src, bna[:, 0:1], st[:, at:at + 1], ALU.subtract, ALU.mult))
                link(tt(scratch, scratch, lnw[:, 2 * which, :], ALU.mult))
                return tt(dst, scratch, lnw[:, 2 * which + 1, :], ALU.add)

            for i in range(NT):
                cols = slice(i * P, (i + 1) * P)
                dve.wait_ge(a_ready, 1)
                tt(Ma, bc(tri, 1, NH), bc(a_sb[:, i, :], 2, P), ALU.mult).then_inc(Ma_ready, 1)
                for half in range(2):
                    await_taken(dve, "xT", i, half)
                heads = lambda ap: ap.rearrange("p (h d) -> p h d", d=HD)
                xi = heads(x_tm[:, i, :])
                tt(heads(xdt), xi, bc(dt[:, i, :], 2, HD), ALU.mult).then_inc(xdt_ready, 1)
                if i == 0:
                    dve.wait_ge(xdt_ready, 1)
                    await_taken(dve, "acs")
                    tt(heads(xdd), heads(xdt), bc(ea[:, 0, 1, :], 2, HD), ALU.mult).then_inc(xdd_ready, 1)
                o = await_full(dve, "cb", i)[:, 0:NG * P].rearrange("p (g l) -> p g l", g=NG)
                taken(tt(CBm[:, :, :], o, bc(tri, 1, NG), ALU.mult), "cb", i)
                await_taken(dve, "cb", i)
                for n in range(4):
                    await_taken(dve, "seg", i, n)
                    e4 = E[:, 4 * n:4 * n + 4, :]
                    tt(e4, e4, bc(CBm[:, n // 2, :], 1, 4), ALU.mult).then_inc(sco_ready, 1)
                y = ymix[:, 0:D]
                link(tt(heads(y), xi, bc(pr[:, 2, :], 2, HD), ALU.mult))
                for g in range(NG):
                    yg = y[:, g * 512:(g + 1) * 512]
                    o = await_full(dve, "yd", i, g)
                    taken(tt(yg, yg, o, ALU.add), "yd", i, g)
                    await_taken(dve, "yd", i, g)
                    if i:
                        o = await_full(dve, "yo", g)
                        t = xdd[:, g * 512:(g + 1) * 512]
                        taken(tt(heads(t), heads(o), bc(ea[:, 1, 0, 8 * g:8 * g + 8], 2, HD), ALU.mult), "yo", g)
                        await_taken(dve, "yo", g)
                        link(tt(yg, yg, t, ALU.add))
                for n in range(2):
                    await_taken(dve, "z", n, i)
                tt(y, y, zs[:, i, :], ALU.mult).then_inc(y_ready, 1)
                dve.wait_ge(y_ready, i + 1)
                rms(0, NG, 512, 2 * i + 1, 3 * i + 1)
                for g in range(NG):
                    last = V.tensor_scalar(y[:, g * 512:(g + 1) * 512], y[:, g * 512:(g + 1) * 512], st[:, g:g + 1], None, ALU.mult)
                link(last)

                for n in range(3):
                    await_taken(dve, "tm", n, i)
                q = heads(tm[:, i, TM_Q:TM_Q + D])
                at = C_ROPE + i * 4 * HD
                qc, qs = cst[:, at:at + HD], cst[:, at + HD:at + 2 * HD]
                tt(qt[:, :, 0:HD // 2], q[:, :, HD // 2:HD], bc(qs[:, 0:HD // 2], 1, NH), ALU.mult)
                tt(qt[:, :, HD // 2:HD], q[:, :, 0:HD // 2], bc(qs[:, HD // 2:HD], 1, NH), ALU.mult)
                link(tt(qr, q, bc(qc, 1, NH), ALU.mult))
                tt(qr, qr, qt, ALU.add).then_inc(qr_ready, 1)
                o = await_full(dve, "sc", i)[:, 0:NH * NCMP].rearrange("p (h n) -> p h n", h=NH)
                bias = cst[:, C_CBIAS + i * NCMP:C_CBIAS + (i + 1) * NCMP]
                valid = cst[:, C_CVALID + i * NCMP:C_CVALID + (i + 1) * NCMP]
                taken(tt(Pe, o, bc(bias, 1, NH), ALU.add), "sc", i)
                await_taken(dve, "sc", i)
                link(V.tensor_reduce(cst1[:, 0, :], Pe, AX, ALU.max))
                tt(Pe, Pe, bc(cst1[:, 0, :], 2, NCMP), ALU.subtract).then_inc(cm_ready, 1)
                dve.wait_ge(ce_ready, i + 1)
                link(V.tensor_reduce(cst1[:, 1, :], Pe, AX, ALU.add))
                dve.wait_ge(sg_ready, 1)
                link(tt(Pe, Pe, bc(valid, 1, NH), ALU.mult))
                link(V.reciprocal(cst1[:, 2, :], cst1[:, 1, :]))
                gates = sg[:, i, :].rearrange("p (h b) -> p h b", b=3)
                link(tt(cst1[:, 3, :], cst1[:, 2, :], gates[:, :, 0], ALU.mult))
                dve.wait_ge(pc_zero, i + 1)
                tt(Pc[:, :, 0:NCMP], Pe, bc(cst1[:, 3, :], 2, NCMP), ALU.mult).then_inc(pc_ready, 1)

                def maxima(u):
                    o = await_full(dve, "S", i, u)
                    V.tensor_reduce(nmx[:, u, :], o.rearrange("p (e t) -> p e t", e=2)[:, :, 0:(i + 1) * P], AX, ALU.max, negate=True).then_inc(nm_ready, 1)

                for u in range(-2, len(UN)):
                    if u + 2 < len(UN):
                        maxima(u + 2)
                    if u >= 0:
                        kv, gp, b = UN[u]
                        h = kv * GQ + 2 * gp
                        await_taken(dve, "S", i, u)
                        link(V.reciprocal(coef[:, u, :], lsum[:, u, :]))
                        link(tt(coef[:, u, :], coef[:, u, :], gates[:, h:h + 2, 1 + b], ALU.mult))
                        for e in range(2):
                            part = Pb[:, u % 3, e, 0:(i + 1) * P]
                            last = V.tensor_scalar(part, part, coef[:, u, e:e + 1], None, ALU.mult)
                        last.then_inc(p_ready, 1)
                dve.wait_ge(pv_done, len(UN) * (i + 1))
                y = ymix[:, D:2 * D]
                for n in range(2):
                    V.tensor_copy(y[:, n * 512:(n + 1) * 512], ps[:, 6 + n, :]).then_inc(o_taken, 1)
                rms(12, 1, D, 2 * i + 2, 3 * i + 2)
                V.tensor_scalar(y, y, st[:, 12:13], None, ALU.mult).then_inc(ymix_ready, 1)

                for n in range(4):
                    o = await_full(dve, "mT", i, n).rearrange("p (c t) -> p c t", c=4)
                    taken(tt(mixT[:, 4 * n:4 * n + 4, :], o, bc(nw[:, 4 * n:4 * n + 4], 2, P), ALU.mult), "mT", i, n)
                dve.wait_ge(x_here, 16)
                for n in range(2):
                    o = await_full(dve, "mix", i, n)
                    part = slice(n * 512, (n + 1) * 512)
                    taken(V.scalar_tensor_tensor(r1[:, part], x_sb[:, i, part], ALPHA, o, ALU.mult, ALU.add), "mix", i, n)
                for n in range(2):
                    await_taken(dve, "mix", i, n)
                dve.wait_ge(ln_here, 64)
                layer_norm(h_sb[:, i, :], r1, junk, 0, 24, 3 * i + 3).then_inc(h_ready, 1)
                for n in range(4):
                    o = await_full(dve, "qpT", i, n).rearrange("p (c t) -> p c t", c=4)
                    taken(V.tensor_copy(qpT[:, 4 * n:4 * n + 4, :], o), "qpT", i, n)

            await_taken(dve, "s", NT - 1, 3)
            for n in range(4):
                await_full(dve, "s", NT - 1, n)
            link(V.memset(zero, 0.0))
            link(V.memset(s_all[:, NT * PH * 2 * NKEY:], 0.0))
            V.memset(gsm[:, 2:3], 0.0).then_inc(zero_ready, 1)
            V.memset(gsm[:, 3:4], 0.0).then_inc(ks_used, 1)
            V.memset(acc2[:, 0:8], 0.0).then_inc(row_used, RING)
            iota = cst[:, C_IOTA:C_IOTA + TOPK]

            def choose(u, par):
                count = [0]

                def step(ins):
                    count[0] += 1
                    ins.then_inc(loop_step, 1)
                    await_alone(dve, dve_passed, loop_step, u * CHOOSE_STEPS + count[0])

                await_alone(dve, dve_passed, ks_ready, u + 1)
                for c in range(2):
                    step(V.max(top[:, c, 0:8], ks[:, c, :]))
                    step(V.max_index(topi[:, c, 0:8], top[:, c, 0:8], ks[:, c, :]))
                    step(V.match_replace(ks2[:, c, :], top[:, c, 0:8], ks[:, c, :], BELOW))
                    step(V.max(top[:, c, 8:16], ks2[:, c, :]))
                    step(V.max_index(topi[:, c, 8:16], top[:, c, 8:16], ks2[:, c, :]))
                V.tensor_copy(topif, topi[:, :, :]).then_inc(ks_used, 1)
                grid = cand.rearrange("p (a b) -> p a b", a=TOPK)
                step(tt(grid, bc(top[:, 0, :], 2, TOPK), bc(top[:, 1, :], 1, TOPK), ALU.add))
                step(V.max(gtop[:, 0:8], cand))
                step(V.max_index(gpos[:, 0, 0:8], gtop[:, 0:8], cand))
                step(V.match_replace(cand2, gtop[:, 0:8], cand, BELOW))
                step(V.max(gtop[:, 8:16], cand2))
                V.tensor_scalar(gsm[:, 0:1], gtop[:, 0:1], -1.0, None, ALU.mult).then_inc(gs_ready, 1)
                step(V.max_index(gpos[:, 0, 8:16], gtop[:, 8:16], cand2))
                V.tensor_scalar(gpos[:, 1, :], gpos[:, 0, :], 4, None, ALU.logical_shift_right)
                step(V.tensor_scalar(gpos[:, 2, :], gpos[:, 0, :], TOPK - 1, None, ALU.bitwise_and))
                step(V.tensor_copy(pij, gpos[:, 1:3, :]))
                cells = lambda ap: ap.rearrange("p (a b) -> p a b", b=TOPK)
                step(tt(cells(hot), bc(pij.rearrange("p c k -> p (c k)"), 2, TOPK), bc(iota, 1, 2 * TOPK), ALU.is_equal))
                for c in range(2):
                    half = slice(c * TOPK * TOPK, (c + 1) * TOPK * TOPK)
                    last = tt(cells(hot2[:, half]), cells(hot[:, half]), bc(topif[:, c, :], 1, TOPK), ALU.mult)
                step(last)
                step(V.tensor_reduce(eij.rearrange("p c k -> p (c k)"), cells(hot2), AX, ALU.add))
                V.scalar_tensor_tensor(eidx[:, par, :], eij[:, 0, :], float(NKEY), eij[:, 1, :], ALU.mult, ALU.add).then_inc(idx_ready, 1)
                dve.wait_ge(ge_ready, u + 1)
                step(V.reciprocal(gsm[:, 2:3], gsm[:, 1:2]))
                step(V.tensor_scalar(gate[:, par, :], gexp, gsm[:, 2:3], None, ALU.mult))
                assert count[0] == CHOOSE_STEPS, count

            def weigh(u, e, k):
                step = e * TOPK + k
                dve.wait_ge(w_step, u * TOPK + (k + 1))
                dve.wait_ge(row_used, u * TOPK + (k + 1 + RING - DIAGS))
                V.tensor_scalar(diag[:, step % DIAGS, :], ident, wact[:, e, 0, k:k + 1], gate[:, e, k:k + 1], ALU.mult, ALU.mult).then_inc(diag_ready, 1)

            choose(0, 0)
            for i in range(NT):
                with dve.Fori(0, PH // 2) as pair:
                    for e in range(2):
                        u = pair * 2 + (i * PH + e)
                        for k in range(TOPK):
                            slot = k % RING
                            dve.wait_ge(row_here[slot], u * (16 * TOPK // RING) + 16 * (k // RING + 1))
                            if not (i == 0 and e == 0 and k == 0):
                                dve.wait_ge(dot_done, u * TOPK + k)
                            V.tensor_tensor_reduce(out=dotj, in0=row(slot)[:, 0:D], in1=h_sb[:, i, :], scale=1.0, scalar=0.0,
                                                   op0=ALU.mult, op1=ALU.add, accum_out=hdot[:, e, k:k + 1]).then_inc(dot_done, 1)
                            if k >= LAG:
                                weigh(u, e, k - LAG)
                            if k == TOPK // 2 - 1:
                                choose(u + 1, 1 - e)
                        for k in range(TOPK - LAG, TOPK):
                            weigh(u, e, k)
                for n in range(2):
                    o = await_full(dve, "y", i, n)
                    part = slice(n * 512, (n + 1) * 512)
                    taken(V.scalar_tensor_tensor(acc2[:, part], h_sb[:, i, part], ALPHA, o, ALU.mult, ALU.add), "y", i, n)
                for n in range(2):
                    await_taken(dve, "y", i, n)
                layer_norm(outb[i], acc2, acc2, 1, 36, 3 * NT + i + 1).then_inc(out_ready, 1)

        @block.gpsimd
        def _(pool):
            G = nc.gpsimd
            steps = [0]

            def link(ins):
                steps[0] += 1
                ins.then_inc(pool_step, 1)
                pool.wait_ge(pool_step, steps[0])

            G.memset(xbcT[:, :, 0:TAPS - 1], 0.0).then_inc(pads_zero, 1)
            G.memset(hTr.rearrange("p c k g n -> p (c k g n)"), 0.0).then_inc(hTr_zero, 1)
            pool.wait_ge(prm_here, 80)
            for c in range(2, 4):
                await_taken(pool, "cmp", c)
            add_position(G, 1).then_inc(X_ready[1], 1)
            pool.wait_ge(c_here, 16)
            for i in range(NT):
                for n in range(3, len(TM_PIECES)):
                    await_taken(pool, "tm", n, i)
                if i:
                    await_full(pool, "q", i - 1, 3)
                    for n in range(2):
                        await_taken(pool, "hT", i - 1, n)
                else:
                    for w in range(2):
                        await_full(pool, "hid", w)
                at = C_ROPE + i * 4 * HD + 2 * HD
                kc, ksin = cst[:, at:at + HD], cst[:, at + HD:at + 2 * HD]
                for b, dst in enumerate((kr, kr2)):
                    src = tm[:, i, TM_KV + 512 * b:TM_KV + 512 * b + NKV * HD].rearrange("p (h d) -> p h d", d=HD)
                    G.tensor_tensor(krt[:, :, 0:HD // 2], src[:, :, HD // 2:HD], bc(ksin[:, 0:HD // 2], 1, NKV), ALU.mult)
                    G.tensor_tensor(krt[:, :, HD // 2:HD], src[:, :, 0:HD // 2], bc(ksin[:, HD // 2:HD], 1, NKV), ALU.mult)
                    link(G.tensor_tensor(dst, src, bc(kc, 1, NKV), ALU.mult))
                    G.tensor_tensor(dst, dst, krt, ALU.add).then_inc(kr_ready, 1)
                    pool.wait_ge(kr_ready, 2 * i + b + 1)
                pool.wait_ge(qr_ready, i + 1)
                G.memset(Pc.rearrange("p h n -> p (h n)"), 0.0).then_inc(pc_zero, 1)

            await_full(pool, "q", NT - 1, 3)
            for i in range(NT):
                with pool.Fori(0, PH // 2) as pair:
                    for e in range(2):
                        u = pair * 2 + (i * PH + e)
                        pool.wait_ge(idx_ready, u + 1)
                        for k in range(TOPK):
                            slot = k % RING
                            await_alone(pool, pool_passed, row_used, u * TOPK + (k + 1))
                            G.indirect_dma_start(row(slot), None, uv, bass.IndirectOffsetOnAxis(eidx[:, e, k:k + 1], 0)).then_inc(row_here[slot], 16)


_INPUTS = ["x", "xT", "w_in", "conv", "prm", "normw", "posT", "w1", "w2", "w_out", "ln", "wq", "skT", "uv", "const"]


def arrange(x, w_in, conv_w, conv_b, dt_bias, a_log, d_skip, ssd_norm_w, cmp_pos_k, cmp_w1_k, cmp_w2_k,
            cmp_pos_v, cmp_w1_v, cmp_w2_v, attn_norm_w, w_out, ln1_g, ln1_b, peer_w_query, peer_sub_keys,
            peer_u, peer_v, ln2_g, ln2_b):
    a = lambda v: np.asarray(v)[0]
    return {
        "x": a(x), "xT": a(x).T, "w_in": a(w_in),
        "conv": np.concatenate([a(conv_w), a(conv_b)[None]]).reshape(TAPS + 1, NCONV, P).transpose(2, 1, 0),
        "prm": np.concatenate([a(dt_bias), a(a_log), a(d_skip)])[None],
        "normw": np.concatenate([a(ssd_norm_w), a(attn_norm_w)]).reshape(2 * KD, P).T,
        "posT": np.stack([a(cmp_pos_k), a(cmp_pos_v)]).reshape(2, CLEN // 2, P).transpose(2, 0, 1),
        "w1": np.stack([a(cmp_w1_k), a(cmp_w1_v)]), "w2": np.stack([a(cmp_w2_k), a(cmp_w2_v)]),
        "w_out": a(w_out), "ln": np.stack([a(ln1_g), a(ln1_b), a(ln2_g), a(ln2_b)]), "wq": a(peer_w_query),
        "skT": a(peer_sub_keys).reshape(2 * PH, NKEY, P).transpose(2, 0, 1),
        "uv": np.concatenate([a(peer_u), a(peer_v)], axis=1), "const": constants(),
    }


def kernel(**inputs):
    import concourse.bacc as bacc
    from concourse.bass_utils import run_bass_kernel_spmd

    nc = bacc.Bacc("TRN2", target_bir_lowering=False, num_devices=1)
    arrays = {f"in_{n}": np.ascontiguousarray(v) for n, v in arrange(**inputs).items()}
    args = [nc.dram_tensor(f"in_{n}", arrays[f"in_{n}"].shape, mybir.dt.float32, kind="ExternalInput").ap() for n in _INPUTS]
    out = nc.dram_tensor("out", (T, D), mybir.dt.float32, kind="ExternalOutput").ap()
    layer(nc, *args, out)
    r = run_bass_kernel_spmd(nc, [arrays], core_ids=[0])
    return r.results[0]["out"].reshape(1, T, D)
```

```python
import math
from contextlib import ExitStack

import numpy as np
import concourse.bass as bass
from concourse import mybir

P = 128
D = 1024
T = 256
NT = T // P
KD = D // P
NH = 16
HD = 64
NG = 2
NKV = 4
GQ = NH // NKV
CONV_C = 1536
NCONV = CONV_C // P
TAPS = 4
NCMP = 15
CSTRIDE = 16
CLEN = 32
CHID = 256
SLOT = 32
PH = 8
NKEY = 128
TOPK = 16
NEXP = NKEY * NKEY
ALPHA = 2 ** 0.25
EPS = 1e-5
NEG = -1e30
BELOW = -3e38

Z0, XBC0, DT0, Q0, KC0, KS0, G0 = 0, 1024, 2560, 2576, 3600, 4112, 5136
W_IN = 5184
TM_PIECES = [(DT0, 347), (DT0 + 347, 347), (DT0 + 694, 346), (KS0, 358), (KS0 + 358, 357), (KS0 + 715, 357)]
TM_W = sum(n for _, n in TM_PIECES)
TM_Q = Q0 - DT0
TM_KV = KC0 - DT0
TM_G = TM_KV + G0 - KS0

C_ID, C_TRI, C_STRICT, C_MASK = 0, 128, 256, 384
C_ROPE = 512
C_CROPE = C_ROPE + NT * 4 * HD
C_CBIAS = C_CROPE + 2 * HD
C_CVALID = C_CBIAS + NT * NCMP
C_IOTA = C_CVALID + NT * NCMP
C_HEAD = C_IOTA + TOPK
C_ALL = C_HEAD + GQ

WSLOTS = 2
WPIECE = 4096
RING = 8
RING0 = 6
ORDER1 = [6, 7, 2, 3, 4, 5, 0, 1]
STEPS = PH * TOPK
PARTS = 14
PART_EVERY = 8
AHEAD = [3, 1]
S_BANKS = [[0, 1, 2, 5], [0, 1]]
GATE_AT = [0, 5]
TAIL_BANKS = [2, 5]
LAG = 1
DIAGS = 4
TAIL_AT = [[0, 1]] + [[part] for part in range(2, PARTS)] + [[]] * 3
CHOICE_AT = [[]] * (PARTS - 1) + [[0, 1], [2, 3], [4, 5, 6]]
CHOOSE_AT = 1
CHOOSE_STEPS = [5, 5, 3, 3, 3, 2, 2]


def constants():
    c = np.zeros((P, C_ALL), np.float32)
    p, f = np.arange(P)[:, None], np.arange(P)[None, :]
    c[:, C_ID:C_ID + P] = p == f
    c[:, C_TRI:C_TRI + P] = p <= f
    c[:, C_STRICT:C_STRICT + P] = p > f
    c[:, C_MASK:C_MASK + P] = np.where(f <= p, 0, NEG)
    inv = np.float32(10000.0) ** (-np.arange(0, HD, 2, dtype=np.float32) / HD)

    def table(pos):
        a = pos.astype(np.float32)[:, None] * inv[None, :]
        cos, sin = np.cos(a), np.sin(a)
        return np.concatenate([cos, cos], 1), np.concatenate([-sin, sin], 1)

    for i in range(NT):
        cos, sin = table(np.arange(P) + i * P)
        at = C_ROPE + i * 4 * HD
        for j, v in enumerate((cos * HD ** -0.5, sin * HD ** -0.5, cos, sin)):
            c[:, at + j * HD:at + (j + 1) * HD] = v
        end = np.arange(NCMP) * CSTRIDE + CLEN - 1
        ok = end[None, :] <= (np.arange(P) + i * P)[:, None]
        c[:, C_CBIAS + i * NCMP:C_CBIAS + (i + 1) * NCMP] = np.where(ok, 0, NEG)
        c[:, C_CVALID + i * NCMP:C_CVALID + (i + 1) * NCMP] = ok
    cos, sin = table(np.arange(NCMP) * CSTRIDE + CLEN - 1)
    c[:NCMP, C_CROPE:C_CROPE + HD] = cos
    c[:NCMP, C_CROPE + HD:C_CROPE + 2 * HD] = sin
    c[:, C_IOTA:C_IOTA + TOPK] = np.arange(TOPK)[None, :]
    c[:, C_HEAD:C_HEAD + GQ] = (np.arange(P)[:, None] // SLOT) == np.arange(GQ)[None, :]
    return c


def units():
    return [(kv, gp, b) for kv in range(NKV) for gp in range(GQ // 2) for b in range(2)]


def bank_plan():
    jobs, turn = {}, [0] * 8

    def add(bank, *name):
        jobs[name] = (bank, turn[bank])
        turn[bank] += 1

    k = 0

    def rotate(*name):
        nonlocal k
        add(k % 6, *name)
        k += 1

    for c in range(NCONV):
        rotate("xbc", c)
    for c in range(4):
        rotate("cmp", c)
    for n in range(len(TM_PIECES)):
        for i in range(NT):
            rotate("tm", n, i)
    for n in range(2):
        for i in range(NT):
            rotate("z", n, i)
    for w in range(2):
        rotate("hid", w)
    for w in range(2):
        rotate("hidT", w)
    rotate("kc")
    rotate("vc")
    rotate("kcT")
    for i in range(NT):
        for half in range(2):
            rotate("xT", i, half)
    rotate("BT")
    rotate("acs")
    for i in range(NT):
        rotate("cb", i)
        for n in range(4):
            rotate("seg", i, n)
        for g in range(NG):
            rotate("yd", i, g)
        for g in range(NG):
            rotate("st" if i == 0 else "yo", g)
    for i in range(NT):
        for n in range(4):
            rotate("qT", i, n)
        for b in range(2):
            rotate("kT", i, b)
        rotate("sc", i)
        add(3, "pcT", i)
        for u in range(len(units())):
            add(S_BANKS[i][u % len(S_BANKS[i])], "S", i, u)
            add(3 + u % 2, "PT", i, u)
    for i in range(NT):
        for name, count in (("mT", 4), ("mix", 2), ("hT", 2), ("q", 4), ("qpT", 4), ("s", 4)):
            for n in range(count):
                if i == 0:
                    add(TAIL_BANKS[n % 2], name, i, n)
                else:
                    rotate(name, i, n)
    for i in range(NT):
        for n in range(2):
            add((6, 4)[i] + n, "y", i, n)
    return jobs


def layer(nc, x, xT, w_in, conv, prm, normw, posT, w1, w2, w_out, ln, wq, skT, uv, const, out):
    fp = mybir.dt.float32
    u32 = mybir.dt.uint32
    ALU = mybir.AluOpType
    ACT = mybir.ActivationFunctionType
    AX = mybir.AxisListType.X
    J = bank_plan()
    UN = units()

    ctx = ExitStack()
    with ctx:
        def sb(name, shape, dt=fp):
            return ctx.enter_context(nc.sbuf_tensor(name, shape, dt))

        def sem(name):
            return ctx.enter_context(nc.semaphore(name))

        cst = sb("cst", [P, C_ALL])
        wring = sb("wring", [P, WSLOTS * WPIECE])
        ring2 = sb("ring2", [P, 2 * 2 * D])
        late = sb("late", [P, NCONV * T + 4 * NT * D - 2 * D + NT * TM_W])
        x_sb = sb("x_sb", [P, NT, D])
        h_sb = sb("h_sb", [P, NT, D])
        B_tm = sb("B_tm", [P, NG, P])
        sk = sb("sk", [P, 2 * PH, NKEY])
        s_all = sb("s_all", [P, (NT * PH + 1) * 2 * NKEY])
        lnw = sb("lnw", [P, 4, D])
        cw = sb("cw", [P, NCONV, TAPS + 1])
        pr = sb("pr", [P, 3, NH])
        nw = sb("nw", [P, 2 * KD])
        pos = sb("pos", [P, 2, CLEN // 2])
        w2s = sb("w2s", [P, 2, 2, HD])
        sg = sb("sg", [P, NT, 3 * NH])
        kcT = sb("kcT", [HD, NKV, NCMP])
        kT = sb("kT", [HD, 2, NKV, T])
        CBm = sb("CBm", [P, NG, P])
        dtb = sb("dtb", [P, 8, NT, NH])
        a_sb = sb("a_sb", [P, NT, NH])
        ea = sb("ea", [P, NT, 2, NH])
        st = sb("st", [P, 64])
        bn = sb("bn", [P, 2, 6])
        bna = sb("bna", [P, 2])
        nmx = sb("nmx", [P, len(UN), 2])
        lsum = sb("lsum", [P, len(UN), 2])
        coef = sb("coef", [P, len(UN), 2])
        cst1 = sb("cst1", [P, 4, NH])

        tmp = sb("tmp", [P, 7664])

        def view(at, *shape, src=None, parts=P):
            size = math.prod(shape)
            v = (tmp if src is None else src)[0:parts, at:at + size]
            if len(shape) == 1:
                return v
            names = "abcd"[:len(shape)]
            kw = {n: s for n, s in zip(names[1:], shape[1:])}
            return v.rearrange(f"p ({' '.join(names)}) -> p {' '.join(names)}", **kw)

        xc = view(0, NCONV, T, src=late)
        at_x = NCONV * T
        x_tm = view(at_x, NT, D, src=late)
        zs = view(at_x + NT * D, NT, D, src=late)
        S0 = view(at_x + 2 * NT * D, D, src=late)
        Vbd = view(at_x + (2 * NT + 1) * D, NKV, GQ, HD, src=late)
        tm = view(at_x + (2 * NT + 2) * D, NT, TM_W, src=late)
        xT_sb = view(0, KD, T)
        xbcT = view(2048, NCONV, T + TAPS - 1)
        kd = view(2048 + NCONV * (T + TAPS - 1), 2, NKV, T)
        flat = s_all
        Xc = view(0, 2, CLEN // 2, NKV * NCMP, src=flat)
        hg = view(1920, 2, CHID, src=flat, parts=NKV * NCMP)
        hTs = view(2432, 2, 2, NKV * NCMP, src=flat)
        hTr = view(2672, 2, NKV, GQ, SLOT, src=flat)
        kcr = view(3696, NKV, HD, src=flat, parts=NCMP)
        kcr2 = view(1920 + 2 * CHID - 512, NKV, HD, src=flat, parts=NCMP)
        Ma = view(0, NH, P)
        E = view(2048, NH, P)
        xdt = view(4096, D)
        xdd = view(5120, D)
        ymixes = [s_all[:, i * 2 * D:(i + 1) * 2 * D] for i in range(NT)]
        qrs = [view(i * D, NH, HD, src=ring2) for i in range(NT)]
        qt = view(NT * D, NH, HD, src=ring2)
        squares = view((NT + 1) * D, D, src=ring2)
        Pb = view(0, max(AHEAD) + 1, 2, T)
        qT = view(2048, NH, P, parts=HD)
        PTs = view(4096, 2, 2, NT, P)
        Pc = view(5120, NH, SLOT)
        Pe = view(5632, NH, NCMP)
        PcT = view(5872, NKV, P)
        kr = view(6384, NKV, HD)
        krt = view(6640, NKV, HD)
        kr2 = view(6896, NKV, HD)
        mixTs = [view(0, 2 * KD, P, src=late), view(0, 2 * KD, P)]
        hTails = [view(2 * KD * P, KD, P, src=late), view(6144, KD, P)]
        qtoks = [view(at_x, 2 * PH * NKEY, src=late), view(0, 2 * PH * NKEY)]
        qpTs = [view(at_x + NT * D, 2 * PH, P, src=late), view(2048, 2 * PH, P)]
        r1s = [view(at_x + 2 * NT * D, D, src=late), view(4096, D)]
        junks = [view(at_x, D, src=late), view(5120, D)]
        at_tm = at_x + (2 * NT + 2) * D
        q_place = [at_tm + i * TM_W + TM_Q for i in range(NT)]
        kv_place = [at_tm + i * TM_W + TM_KV for i in range(NT)]
        hot = view(q_place[0], 2 * TOPK * TOPK, src=late)
        hot2 = view(q_place[0] + 512, 2 * TOPK * TOPK, src=late)
        ks = view(q_place[1] + 0, 2, NKEY, src=late)
        ks2 = view(q_place[1] + 256, 2, NKEY, src=late)
        cand = view(q_place[1] + 512, TOPK * TOPK, src=late)
        cand2 = view(q_place[1] + 768, TOPK * TOPK, src=late)
        top = view(kv_place[0] + 0, 2, TOPK, src=late)
        topif = view(kv_place[0] + 32, 2, TOPK, src=late)
        gtop = view(kv_place[0] + 64, TOPK, src=late)
        pij = view(kv_place[0] + 80, 2, TOPK, src=late)
        eij = view(kv_place[0] + 112, 2, TOPK, src=late)
        gexp = view(kv_place[0] + 144, TOPK, src=late)
        gate = view(kv_place[0] + 160, 2, TOPK, src=late)
        gsm = view(kv_place[0] + 192, 4, src=late)
        zero = view(kv_place[0] + 512, P, src=late)
        dotj = view(at_x + (2 * NT + 1) * D, D, src=late)
        hdot = view(kv_place[0] + 256, 2, TOPK, src=late)
        wact = view(kv_place[0] + 256 + 32, 2, 2, TOPK, src=late)
        diag = view(kv_place[1] + 256, DIAGS, P, src=late)
        acc2 = view(4096, D)
        outb = [view(5120, D), view(6144, D)]
        topi = sb("topi", [P, 2, TOPK], u32)
        gpos = sb("gpos", [P, 3, TOPK], u32)
        eidx = sb("eidx", [P, 2, TOPK], u32)

        ps = ctx.enter_context(nc.psum_tensor("ps", [P, 8, 512], fp))

        ident = cst[:, C_ID:C_ID + P]
        tri = cst[:, C_TRI:C_TRI + P]
        strict = cst[:, C_STRICT:C_STRICT + P]
        cmask = cst[:, C_MASK:C_MASK + P]

        full = [sem(f"bank{b}_full") for b in range(8)]
        free = [sem(f"bank{b}_free") for b in range(8)]
        w_here = [sem(f"w_here{s}") for s in range(WSLOTS)]
        first_here = [sem(f"first_here{c}") for c in range(4)]
        c_here = sem("c_here")
        x_here = sem("x_here")
        xT_here = sem("xT_here")
        prm_here = sem("prm_here")
        sk_here = sem("sk_here")
        ln_here = sem("ln_here")
        dve_step = sem("dve_step")
        act_step = sem("act_step")
        pool_step = sem("pool_step")
        wout_used = sem("wout_used")
        pads_zero = sem("pads_zero")
        conv_done = sem("conv_done")
        silu_done = sem("silu_done")
        X_ready = [sem("Xk_ready"), sem("Xv_ready")]
        hTr_ready = sem("hTr_ready")
        hTr_zero = sem("hTr_zero")
        dt_in = sem("dt_in")
        dt_ln = sem("dt_ln")
        a_ready = sem("a_ready")
        Ma_ready = sem("Ma_ready")
        sco_ready = sem("sco_ready")
        xdt_ready = sem("xdt_ready")
        xdd_ready = sem("xdd_ready")
        y_ready = sem("y_ready")
        sq_ready = sem("sq_ready")
        ms_ready = sem("ms_ready")
        sd_ready = sem("sd_ready")
        qr_ready = sem("qr_ready")
        kr_ready = sem("kr_ready")
        ssd_used = sem("ssd_used")
        sg_ready = sem("sg_ready")
        cm_ready = sem("cm_ready")
        ce_ready = sem("ce_ready")
        pc_ready = sem("pc_ready")
        nm_ready = sem("nm_ready")
        p_ready = sem("p_ready")
        pv_done = sem("pv_done")
        o_taken = sem("o_taken")
        kcr_ready = sem("kcr_ready")
        pc_zero = sem("pc_zero")
        loop_step = sem("loop_step")
        dve_passed = sem("dve_passed")
        pool_passed = sem("pool_passed")
        ymix_ready = sem("ymix_ready")
        h_ready = sem("h_ready")
        ks_ready = sem("ks_ready")
        ks_used = sem("ks_used")
        gs_ready = sem("gs_ready")
        ge_ready = sem("ge_ready")
        idx_ready = sem("idx_ready")
        row_here = [sem(f"row_here{s}") for s in range(RING)]
        row_used = sem("row_used")
        dot_done = sem("dot_done")
        w_step = sem("w_step")
        diag_ready = sem("diag_ready")
        zero_ready = sem("zero_ready")
        out_ready = sem("out_ready")
        out_done = sem("out_done")

        def row(slot):
            src, n = ((late, slot), (ring2, slot - 4), (wring, slot - 6))[(slot >= 4) + (slot >= 6)]
            return src[:, n * 2 * D:(n + 1) * 2 * D]

        def place(i, k):
            return k % RING0 if i == 0 else ORDER1[k % RING]

        def arrivals(i, pair, k):
            if i == 0:
                return (pair * 2 * TOPK + k) // RING0 + 1
            before = len(range(place(1, k), STEPS, RING0)) if place(1, k) < RING0 else 0
            return pair * (2 * TOPK // RING) + (before + k // RING + 1)

        def await_full(eng, *name):
            b, n = J[name]
            eng.wait_ge(full[b], n + 1)
            return ps[:, b, :]

        def await_free(eng, *name):
            b, n = J[name]
            if n:
                eng.wait_ge(free[b], n)
            return ps[:, b, :]

        def await_taken(eng, *name):
            b, n = J[name]
            eng.wait_ge(free[b], n + 1)

        def taken(ins, *name):
            ins.then_inc(free[J[name][0]], 1)

        def filled(ins, *name):
            ins.then_inc(full[J[name][0]], 1)

        def await_alone(eng, passed, what, value):
            eng.wait_ge(what, value)
            if not isinstance(value, int):
                eng.sem_inc(passed, 1)

        def bc(ap, axis, n):
            ap = ap.unsqueeze(axis)
            shape = list(ap.shape)
            shape[axis] = n
            return ap.to_broadcast(shape)

        def add_position(eng, w):
            half = CSTRIDE // 2
            for kv in range(NKV):
                for m in range(2):
                    pairs = kd[:, w, kv, m * CSTRIDE:(m + NCMP) * CSTRIDE].rearrange("p (n c j) -> p j c n", c=half, j=2)[:, 0, :, :]
                    rows = slice(m * half, (m + 1) * half)
                    last = eng.tensor_tensor(Xc[:, w, rows, kv * NCMP:(kv + 1) * NCMP], pairs, bc(pos[:, w, rows], 2, NCMP), ALU.add)
            return last

        pieces = []
        for n in range(3):
            pieces.append((w_in[:, XBC0 + 512 * n:XBC0 + 512 * (n + 1)], 512, ("xbc", 4 * n + 3)))
        pieces.append((w_in[:, KC0:KS0], 512, ("cmp", 3)))
        for n, (at, w) in enumerate(TM_PIECES):
            pieces.append((w_in[:, at:at + w], w, ("tm", n, NT - 1)))
        for n in range(2):
            pieces.append((w_in[:, Z0 + 512 * n:Z0 + 512 * (n + 1)], 512, ("z", n, NT - 1)))
        for w in range(2):
            pieces.append((w1[w], CHID, ("hid", w)))
        for i in range(NT):
            for n in range(4):
                pieces.append((w_out[512 * n:512 * (n + 1), :], D, 3 * i + n + 1 if n < 3 else ("mix", i, 1)))
            for n in range(4):
                pieces.append((wq[:, 512 * n:512 * (n + 1)], 512, ("q", i, n)))
        piece_no = iter(range(len(pieces)))

        def piece_view(k):
            src, n, _ = pieces[k]
            rows = src.shape[0] // P
            at = (k % WSLOTS) * WPIECE
            return wring[:, at:at + rows * n].rearrange("p (k n) -> p k n", k=rows)

        block = ctx.enter_context(nc.Block())

        @block.sync
        def _(sp):
            for k, (src, n, _) in enumerate(pieces):
                if k == 2:
                    sp.dma_start(cst[:, :], const).then_inc(c_here, 16)
                    sp.dma_start(cw[:, :, :], conv).then_inc(prm_here, 16)
                    sp.dma_start(pr[:, :, :].rearrange("p a n -> p (a n)"), prm.to_broadcast([P, 3 * NH])).then_inc(prm_here, 16)
                    sp.dma_start(nw[:, :], normw).then_inc(prm_here, 16)
                    sp.dma_start(pos[:, :, :], posT).then_inc(prm_here, 16)
                    sp.dma_start(w2s[:, :, :, :].rearrange("p w c n -> p (w c) n"), w2.rearrange("w (c p) n -> p (w c) n", p=P)).then_inc(prm_here, 16)
                if k == 12:
                    sp.dma_start(x_sb[:, :, :], x.rearrange("(i p) n -> p i n", p=P)).then_inc(x_here, 16)
                    sp.dma_start(sk[:, :, :], skT).then_inc(sk_here, 16)
                    for j in range(4):
                        sp.dma_start(lnw[:, j, :], ln[j:j + 1, :].to_broadcast([P, D])).then_inc(ln_here, 16)
                if k >= WSLOTS:
                    end = pieces[k - WSLOTS][2]
                    if isinstance(end, int):
                        sp.wait_ge(wout_used, end)
                    else:
                        await_full(sp, *end)
                if k == 0:
                    for c in range(4):
                        sp.dma_start(piece_view(0)[:, :, c * P:(c + 1) * P], src[:, c * P:(c + 1) * P].rearrange("(k p) n -> p k n", p=P)).then_inc(first_here[c], 16)
                        if c == 0:
                            sp.dma_start(xT_sb, xT.rearrange("(k p) t -> p k t", p=P)).then_inc(xT_here, 16)
                else:
                    sp.dma_start(piece_view(k), src.rearrange("(k p) n -> p k n", p=P)).then_inc(w_here[k % WSLOTS], 16)
            for i in range(NT):
                sp.wait_ge(out_ready, i + 1)
                sp.dma_start(out[i * P:(i + 1) * P, :], outb[i]).then_inc(out_done, 16)
            sp.wait_ge(out_done, 16 * NT)

        @block.tensor
        def _(pe):
            mm = nc.tensor.matmul
            tr = nc.tensor.transpose

            def next_piece():
                k = next(piece_no)
                if k:
                    pe.wait_ge(w_here[k % WSLOTS], 16 * (k // WSLOTS + k % WSLOTS))
                return piece_view(k)

            pe.wait_ge(xT_here, 16)
            for kind, count in (("xbc", NCONV), ("cmp", 4)):
                for c in range(count):
                    if c % 4 == 0:
                        w = next_piece()
                    o = await_free(pe, kind, c)
                    if kind == "xbc" and c < 4:
                        pe.wait_ge(first_here[c], 16)
                    for k in range(KD):
                        last = mm(o[:, 0:T], w[:, k, (c % 4) * P:(c % 4 + 1) * P], xT_sb[:, k, :], start=k == 0, stop=k == KD - 1)
                    filled(last, kind, c)
            for kind, widths in (("tm", [n for _, n in TM_PIECES]), ("z", [512, 512])):
                for n, width in enumerate(widths):
                    w = next_piece()
                    for i in range(NT):
                        o = await_free(pe, kind, n, i)
                        for k in range(KD):
                            last = mm(o[:, 0:width], xT_sb[:, k, i * P:(i + 1) * P], w[:, k, :], start=k == 0, stop=k == KD - 1)
                        filled(last, kind, n, i)

            pe.wait_ge(c_here, 16)
            for w in range(2):
                wt = next_piece()
                pe.wait_ge(X_ready[w], 1)
                o = await_free(pe, "hid", w)
                for c in range(CLEN // 2):
                    last = mm(o[0:NKV * NCMP, 0:CHID], Xc[:, w, c, :], wt[:, c, :], start=c == 0, stop=c == CLEN // 2 - 1)
                filled(last, "hid", w)
            for w in range(2):
                await_taken(pe, "hid", w)
                o = await_free(pe, "hidT", w)
                for c in range(2):
                    last = tr(o[:, c * NKV * NCMP:(c + 1) * NKV * NCMP], hg[:, w, c * P:(c + 1) * P], ident[0:NKV * NCMP, 0:NKV * NCMP])
                filled(last, "hidT", w)
            await_taken(pe, "hidT", 0)
            pe.wait_ge(prm_here, 80)
            o = await_free(pe, "kc")
            for kv in range(NKV):
                for c in range(2):
                    last = mm(o[0:NCMP, kv * HD:(kv + 1) * HD], hTs[:, 0, c, kv * NCMP:(kv + 1) * NCMP], w2s[:, 0, c, :], start=c == 0, stop=c == 1)
            filled(last, "kc")
            pe.wait_ge(hTr_ready, 1)
            o = await_free(pe, "vc")
            for kv in range(NKV):
                for c in range(2):
                    last = mm(o[:, kv * HD:(kv + 1) * HD], hTr[:, c, kv, :, :].rearrange("p g n -> p (g n)"), w2s[:, 1, c, :], start=c == 0, stop=c == 1)
            filled(last, "vc")
            pe.wait_ge(kcr_ready, 1)
            o = await_free(pe, "kcT")
            for kv in range(NKV):
                last = tr(o[0:HD, kv * NCMP:(kv + 1) * NCMP], kcr[:, kv, :], ident[0:NCMP, 0:NCMP])
            filled(last, "kcT")

            pe.wait_ge(silu_done, 3)
            for i in range(NT):
                for half in range(2):
                    o = await_free(pe, "xT", i, half)
                    for c in range(4):
                        last = tr(o[:, c * P:(c + 1) * P], xc[:, 4 * half + c, i * P:(i + 1) * P], ident)
                    filled(last, "xT", i, half)
            o = await_free(pe, "BT")
            for g in range(NG):
                last = tr(o[:, g * P:(g + 1) * P], xc[:, KD + g, 0:P], ident)
            filled(last, "BT")
            pe.wait_ge(a_ready, 1)
            o = await_free(pe, "acs")
            for i in range(NT):
                for n, m in enumerate((tri, strict)):
                    at = (2 * i + n) * NH
                    last = mm(o[:, at:at + NH], m, a_sb[:, i, :], start=True, stop=True)
            filled(last, "acs")

            for i in range(NT):
                cols = slice(i * P, (i + 1) * P)
                o = await_free(pe, "cb", i)
                for g in range(NG):
                    last = mm(o[:, g * P:(g + 1) * P], xc[:, KD + g, cols], xc[:, KD + NG + g, cols], start=True, stop=True)
                filled(last, "cb", i)
                pe.wait_ge(Ma_ready, i + 1)
                for n in range(4):
                    o = await_free(pe, "seg", i, n)
                    filled(mm(o, strict, Ma[:, 4 * n:4 * n + 4, :].rearrange("p h l -> p (h l)"), start=True, stop=True), "seg", i, n)
                pe.wait_ge(xdt_ready, i + 1)
                for g in range(NG):
                    o = await_free(pe, "yd", i, g)
                    for k in range(NH // NG):
                        h = g * NH // NG + k
                        if k % 4 == 0:
                            pe.wait_ge(sco_ready, 4 * i + h // 4 + 1)
                        last = mm(o[:, k * HD:(k + 1) * HD], E[:, h, :], xdt[:, h * HD:(h + 1) * HD], start=True, stop=True)
                    filled(last, "yd", i, g)
                if i == 0:
                    pe.wait_ge(xdd_ready, 1)
                    await_taken(pe, "BT")
                    for g in range(NG):
                        o = await_free(pe, "st", g)
                        filled(mm(o, B_tm[:, g, :], xdd[:, g * 512:(g + 1) * 512], start=True, stop=True), "st", g)
                else:
                    for g in range(NG):
                        await_taken(pe, "st", g)
                        o = await_free(pe, "yo", g)
                        filled(mm(o, xc[:, KD + NG + g, cols], S0[:, g * 512:(g + 1) * 512], start=True, stop=True), "yo", g)

            mix = [None, None]

            def tail(i, part):
                if part == 0:
                    pe.wait_ge(ymix_ready, i + 1)
                    for n in range(4):
                        o = await_free(pe, "mT", i, n)
                        for c in range(4):
                            last = tr(o[:, c * P:(c + 1) * P], ymixes[i][:, (4 * n + c) * P:(4 * n + c + 1) * P], ident)
                        filled(last, "mT", i, n)
                elif part <= 4:
                    n = part - 1
                    if n == 0:
                        mix[:] = [await_free(pe, "mix", i, half) for half in range(2)]
                    w = next_piece()
                    await_taken(pe, "mT", i, n)
                    for c in range(4):
                        for half in range(2):
                            last = mm(mix[half], mixTs[i][:, 4 * n + c, :], w[:, c, half * 512:(half + 1) * 512], start=n + c == 0, stop=n + c == 6)
                            if n + c == 6:
                                filled(last, "mix", i, half)
                    if n < 3:
                        last.then_inc(wout_used, 1)
                elif part == 7:
                    pe.wait_ge(h_ready, i + 1)
                    for n in range(2):
                        o = await_free(pe, "hT", i, n)
                        for c in range(4):
                            last = tr(o[:, c * P:(c + 1) * P], h_sb[:, i, (4 * n + c) * P:(4 * n + c + 1) * P], ident)
                        filled(last, "hT", i, n)
                elif 8 <= part <= 11:
                    n = part - 8
                    if n == 0:
                        for half in range(2):
                            await_taken(pe, "hT", i, half)
                    w = next_piece()
                    o = await_free(pe, "q", i, n)
                    for k in range(KD):
                        last = mm(o, hTails[i][:, k, :], w[:, k, :], start=k == 0, stop=k == KD - 1)
                    filled(last, "q", i, n)
                elif part == 12:
                    for n in range(4):
                        await_taken(pe, "q", i, n)
                        o = await_free(pe, "qpT", i, n)
                        for c in range(4):
                            last = tr(o[:, c * P:(c + 1) * P], qtoks[i][:, (4 * n + c) * P:(4 * n + c + 1) * P], ident)
                        filled(last, "qpT", i, n)
                elif part == 13:
                    pe.wait_ge(sk_here, 16)
                    for n in range(4):
                        await_taken(pe, "qpT", i, n)
                        o = await_free(pe, "s", i, n)
                        for c in range(4):
                            last = mm(o[:, c * NKEY:(c + 1) * NKEY], qpTs[i][:, 4 * n + c, :], sk[:, 4 * n + c, :], start=True, stop=True)
                        filled(last, "s", i, n)

            for i in range(NT):
                pe.wait_ge(qr_ready, i + 1)
                for n in range(4):
                    o = await_free(pe, "qT", i, n)
                    for g in range(4):
                        last = tr(o[0:HD, g * P:(g + 1) * P], qrs[i][:, 4 * n + g, :], ident)
                    filled(last, "qT", i, n)
                for b in range(2):
                    pe.wait_ge(kr_ready, 2 * i + b + 1)
                    o = await_free(pe, "kT", i, b)
                    src = kr if b == 0 else kr2
                    for kv in range(NKV):
                        last = tr(o[0:HD, kv * P:(kv + 1) * P], src[:, kv, :], ident)
                    filled(last, "kT", i, b)
                for n in range(4):
                    await_taken(pe, "qT", i, n)
                if i == 0:
                    await_taken(pe, "kcT")
                o = await_free(pe, "sc", i)
                for h in range(NH):
                    last = mm(o[:, h * NCMP:(h + 1) * NCMP], qT[:, h, :], kcT[:, h // GQ, :], start=True, stop=True)
                filled(last, "sc", i)
                for b in range(2):
                    await_taken(pe, "kT", i, b)

                def scores(u):
                    kv, gp, b = UN[u]
                    o = await_free(pe, "S", i, u)
                    for e in range(2):
                        h = kv * GQ + 2 * gp + e
                        n = (i + 1) * P
                        mm(o[:, e * T:e * T + n], qT[:, h, :], kT[:, b, kv, 0:n], start=True, stop=False, skip_group_check=True)
                        last = mm(o[:, e * T + i * P:e * T + n], ident, cmask, start=False, stop=True, skip_group_check=True)
                    filled(last, "S", i, u)

                def values(u):
                    kv, gp, b = UN[u]
                    await_taken(pe, "PT", i, u)
                    for e in range(2):
                        h = kv * GQ + 2 * gp + e
                        o = ps[:, 6 + h // 8, (h % 8) * HD:(h % 8 + 1) * HD]
                        for j in range(i + 1):
                            v = tm[:, j, TM_KV + 256 + 512 * b + kv * HD:TM_KV + 256 + 512 * b + (kv + 1) * HD]
                            last = mm(o, PTs[:, u % 2, e, j, :], v, start=False, stop=b == 1 and j == i, skip_group_check=True)
                    last.then_inc(pv_done, 1)

                if i:
                    pe.wait_ge(o_taken, 2 * i)
                else:
                    await_taken(pe, "vc")
                ahead = AHEAD[i]
                for u in range(-ahead, len(UN) + 1):
                    if u == 0:
                        pe.wait_ge(pc_ready, i + 1)
                        o = await_free(pe, "pcT", i)
                        for kv in range(NKV):
                            last = tr(o[:, kv * P:(kv + 1) * P], Pc[:, kv * GQ:(kv + 1) * GQ, :].rearrange("p g n -> p (g n)"), ident)
                        filled(last, "pcT", i)
                    if 0 <= u + ahead < len(UN):
                        scores(u + ahead)
                    if 0 <= u < len(UN):
                        pe.wait_ge(p_ready, len(UN) * i + u + 1)
                        o = await_free(pe, "PT", i, u)
                        for e in range(2):
                            for j in range(i + 1):
                                last = tr(o[:, (2 * e + j) * P:(2 * e + j + 1) * P], Pb[:, u % (AHEAD[i] + 1), e, j * P:(j + 1) * P], ident)
                        filled(last, "PT", i, u)
                    if u >= 1:
                        if (u - 1) % 4 == 0:
                            kv = (u - 1) // 4
                            if kv == 0:
                                await_taken(pe, "pcT", i)
                            mm(ps[:, 6 + kv // 2, (kv % 2) * GQ * HD:(kv % 2 + 1) * GQ * HD], PcT[:, kv, :],
                               Vbd[:, kv, :, :].rearrange("p g n -> p (g n)"), start=True, stop=False, skip_group_check=True)
                        values(u - 1)
                    if i == 1 and 0 <= u < len(UN):
                        for part in TAIL_AT[u]:
                            tail(0, part)

            def weighted(i, pair, k, o):
                pe.wait_ge(diag_ready, pair * (2 * TOPK) + (STEPS * i + k + 1))
                v_row = row(place(i, pair * 2 * TOPK + k if i == 0 else k))[:, D:2 * D]
                for n in range(2):
                    last = mm(o[n], diag[:, k % DIAGS, :], v_row[:, n * 512:(n + 1) * 512], start=False, stop=False, skip_group_check=True)
                last.then_inc(row_used, 1)

            pe.wait_ge(zero_ready, 1)
            pe.wait_ge(o_taken, 2 * NT)
            nothing = sk[:, 0:4, :].rearrange("p a b -> p (a b)")
            for i in range(NT):
                o = [await_free(pe, "y", i, n) for n in range(2)]
                for n in range(2):
                    mm(o[n], zero, nothing, start=True, stop=False, skip_group_check=True)
                if i == 0:
                    for k in range(STEPS):
                        weighted(0, k // (2 * TOPK), k % (2 * TOPK), o)
                        if (k + 1) % PART_EVERY == 0 and k // PART_EVERY < PARTS:
                            tail(1, k // PART_EVERY)
                else:
                    with pe.Fori(0, PH // 2) as pair:
                        for k in range(2 * TOPK):
                            weighted(1, pair, k, o)
                for n in range(2):
                    filled(mm(o[n], zero, nothing, start=False, stop=True, skip_group_check=True), "y", i, n)

        @block.scalar
        def _(act):
            steps = [0]

            def f(out, in_, func, **kw):
                return nc.scalar.activation(out, in_, func, **kw)

            def link(ins):
                steps[0] += 1
                ins.then_inc(act_step, 1)
                act.wait_ge(act_step, steps[0])

            act.wait_ge(pads_zero, 1)
            for c in range(NCONV):
                o = await_full(act, "xbc", c)
                taken(f(xbcT[:, c, TAPS - 1:], o[:, 0:T], ACT.Copy), "xbc", c)
            for c in range(4):
                o = await_full(act, "cmp", c)
                w, kv = c // 2, 2 * (c % 2)
                for e in range(2):
                    rows = slice(e * HD, (e + 1) * HD)
                    f(kd[0:HD, w, kv + e, :], o[rows, 0:T], ACT.Copy)
                    last = f(kd[HD:P, w, kv + e, 0:T - 1], o[rows, 1:T], ACT.Copy)
                taken(last, "cmp", c)
            at = 0
            for n, (_, width) in enumerate(TM_PIECES):
                for i in range(NT):
                    o = await_full(act, "tm", n, i)
                    taken(f(tm[:, i, at:at + width], o[:, 0:width], ACT.Copy), "tm", n, i)
                at += width
            for n in range(2):
                for i in range(NT):
                    o = await_full(act, "z", n, i)
                    taken(f(zs[:, i, n * 512:(n + 1) * 512], o, ACT.Silu), "z", n, i)
            for n in range(3):
                act.wait_ge(conv_done, 4 * (n + 1))
                f(xc[:, 4 * n:4 * n + 4, :], xc[:, 4 * n:4 * n + 4, :], ACT.Silu).then_inc(silu_done, 1)
            act.wait_ge(dt_in, 1)
            link(f(dtb[:, 2, :, :], dtb[:, 1, :, :], ACT.Exp))
            f(dtb[:, 7, 0, :], pr[:, 1, :], ACT.Exp)
            f(dtb[:, 3, :, :], dtb[:, 2, :, :], ACT.Ln, bias=1.0).then_inc(dt_ln, 1)
            for w in range(2):
                o = await_full(act, "hid", w)
                taken(f(hg[:, w, :], o[0:NKV * NCMP, 0:CHID], ACT.Gelu), "hid", w)
            for w in range(2):
                o = await_full(act, "hidT", w)
                taken(f(hTs[:, w, :, :], o[:, 0:2 * NKV * NCMP].rearrange("p (c n) -> p c n", c=2), ACT.Copy), "hidT", w)
            o = await_full(act, "kcT")
            taken(f(kcT[:, :, :], o[0:HD, 0:NKV * NCMP].rearrange("p (k n) -> p k n", k=NKV), ACT.Copy), "kcT")
            for i in range(NT):
                for half in range(2):
                    o = await_full(act, "xT", i, half)
                    taken(f(x_tm[:, i, half * 512:(half + 1) * 512], o, ACT.Copy), "xT", i, half)
            o = await_full(act, "BT")
            taken(f(B_tm[:, :, :], o[:, 0:NG * P].rearrange("p (g n) -> p g n", g=NG), ACT.Copy), "BT")
            o = await_full(act, "acs")
            taken(f(ea[:, :, :, :], o[:, 0:NT * 2 * NH].rearrange("p (i n h) -> p i n h", i=NT, n=2), ACT.Exp), "acs")
            f(sg[:, :, :], tm[:, :, TM_G:TM_G + 3 * NH], ACT.Sigmoid).then_inc(sg_ready, 1)

            def rms_sum(src, n, width, at, scratch=squares):
                for g in range(n):
                    last = f(scratch[:, g * width:(g + 1) * width], src[:, g * width:(g + 1) * width], ACT.Square, accum_out=st[:, at + g:at + g + 1])
                last.then_inc(sq_ready, 1)

            def root(at, n, value):
                act.wait_ge(ms_ready, value)
                f(st[:, at + 8:at + 8 + n], st[:, at + 4:at + 4 + n], ACT.Sqrt).then_inc(sd_ready, 1)

            def ssd_gate(i):
                act.wait_ge(y_ready, i + 1)
                rms_sum(ymixes[i], NG, 512, 0)

            def ssd_norm(i):
                root(0, NG, i + 1)

            def attention_norm(i):
                act.wait_ge(o_taken, 2 * (i + 1))
                rms_sum(ymixes[i][:, D:2 * D], 1, D, 12, squares if i < NT - 1 else xdd)
                root(12, 1, NT + 2 * i + 1)

            for i in range(NT):
                for n in range(4):
                    o = await_full(act, "seg", i, n)
                    taken(f(E[:, 4 * n:4 * n + 4, :], o.rearrange("p (h l) -> p h l", h=4), ACT.Exp), "seg", i, n)
                if i == 0:
                    for g in range(NG):
                        o = await_full(act, "st", g)
                        taken(f(S0[:, g * 512:(g + 1) * 512], o, ACT.Copy), "st", g)
            def tail(i, part):
                if part == 5:
                    root(24, 1, NT + 2 * i + 2)
                elif part == 7:
                    for n in range(2):
                        o = await_full(act, "hT", i, n)
                        taken(f(hTails[i][:, 4 * n:4 * n + 4, :], o.rearrange("p (h t) -> p h t", h=4), ACT.Copy), "hT", i, n)
                elif 8 <= part <= 11:
                    n = part - 8
                    o = await_full(act, "q", i, n)
                    taken(f(qtoks[i][:, n * 512:(n + 1) * 512], o, ACT.Copy), "q", i, n)
                elif part == 13:
                    for n in range(4):
                        o = await_full(act, "s", i, n)
                        at = i * PH * 2 * NKEY + n * 512
                        taken(f(s_all[:, at:at + 512], o, ACT.Copy), "s", i, n)

            def head_scores(u):
                act.wait_ge(ks_used, u + 1)
                nc.scalar.copy(ks.rearrange("p c n -> p (c n)"), s_all[:, bass.ds(u * (2 * NKEY), 2 * NKEY)]).then_inc(ks_ready, 1)

            def soft(u):
                act.wait_ge(gs_ready, u + 1)
                f(gexp, gtop, ACT.Exp, bias=gsm[:, 0:1], accum_out=gsm[:, 1:2]).then_inc(ge_ready, 1)

            for i in range(NT):
                for n in range(4):
                    o = await_full(act, "qT", i, n)
                    taken(f(qT[:, 4 * n:4 * n + 4, :], o[0:HD, :].rearrange("p (h t) -> p h t", h=4), ACT.Copy), "qT", i, n)
                for b in range(2):
                    o = await_full(act, "kT", i, b)
                    taken(f(kT[:, b, :, i * P:(i + 1) * P], o[0:HD, :].rearrange("p (h t) -> p h t", h=NKV), ACT.Copy), "kT", i, b)
                act.wait_ge(cm_ready, i + 1)
                f(Pe, Pe, ACT.Exp).then_inc(ce_ready, 1)
                if i:
                    attention_norm(i - 1)

                ahead = AHEAD[i]

                def exps(u):
                    n = (i + 1) * P
                    act.wait_ge(nm_ready, len(UN) * i + u + 1)
                    o = await_full(act, "S", i, u)
                    if u > ahead:
                        await_full(act, "PT", i, u - ahead - 1)
                    for e in range(2):
                        last = f(Pb[:, u % (ahead + 1), e, 0:n], o[:, e * T:e * T + n], ACT.Exp, bias=nmx[:, u, e:e + 1], accum_out=lsum[:, u, e:e + 1])
                    taken(last, "S", i, u)

                for u in range(-ahead, len(UN)):
                    if u == 0:
                        o = await_full(act, "pcT", i)
                        taken(f(PcT, o.rearrange("p (h t) -> p h t", h=NKV), ACT.Copy), "pcT", i)
                    if u >= 0:
                        o = await_full(act, "PT", i, u)
                        if u >= 2:
                            act.wait_ge(pv_done, len(UN) * i + u - 1)
                        taken(f(PTs[:, u % 2, :, 0:i + 1, :], o.rearrange("p (e j t) -> p e j t", e=2, j=NT)[:, :, 0:i + 1, :], ACT.Copy), "PT", i, u)
                    if u + ahead < len(UN):
                        exps(u + ahead)
                    if i == 0 and u in GATE_AT:
                        ssd_gate(GATE_AT.index(u))
                    if i == 0 and u - 1 in GATE_AT:
                        ssd_norm(GATE_AT.index(u - 1))
                    if i == 1 and u >= 0:
                        for part in TAIL_AT[u]:
                            tail(0, part)
                        if 0 in CHOICE_AT[u]:
                            act.wait_ge(zero_ready, 1)
                            head_scores(0)
                        if 3 in CHOICE_AT[u]:
                            soft(0)
                if i == NT - 1:
                    attention_norm(i)


            def head(i, u, e):
                if i == 0 and u == PH - 1:
                    for n in range(4):
                        await_taken(act, "s", 1, n)
                head_scores(u + 1)
                for k in range(TOPK):
                    act.wait_ge(dot_done, u * TOPK + (k + 1))
                    f(wact[:, e, 0, k:k + 1], hdot[:, e, k:k + 1], ACT.Gelu).then_inc(w_step, 1)
                    if k == CHOOSE_AT + 3:
                        soft(u + 1)
                    if i == 0 and (k + 1) % PART_EVERY == 0 and (u * TOPK + k) // PART_EVERY < PARTS:
                        tail(1, (u * TOPK + k) // PART_EVERY)

            for u in range(PH):
                head(0, u, u % 2)
            root(36, 1, 3 * NT + 1)
            with act.Fori(0, PH // 2) as pair:
                for e in range(2):
                    head(1, pair * 2 + (PH + e), e)
            root(36, 1, 3 * NT + 2)

        @block.vector
        def _(dve):
            V = nc.vector
            steps = [0]

            def link(ins):
                steps[0] += 1
                ins.then_inc(dve_step, 1)
                dve.wait_ge(dve_step, steps[0])

            def tt(out, a, b, op):
                return V.tensor_tensor(out, a, b, op)

            dve.wait_ge(prm_here, 80)
            for c in range(NCONV):
                await_taken(dve, "xbc", c)
                link(V.tensor_scalar(xc[:, c, :], xbcT[:, c, 0:T], cw[:, c, 0:1], cw[:, c, TAPS:TAPS + 1], ALU.mult, ALU.add))
                for k in range(1, TAPS):
                    ins = V.scalar_tensor_tensor(xc[:, c, :], xbcT[:, c, k:k + T], cw[:, c, k:k + 1], xc[:, c, :], ALU.mult, ALU.add)
                    if k < TAPS - 1:
                        link(ins)
                    else:
                        ins.then_inc(conv_done, 1)
            for c in range(2):
                await_taken(dve, "cmp", c)
            add_position(V, 0).then_inc(X_ready[0], 1)
            for i in range(NT):
                await_taken(dve, "tm", 0, i)
            link(tt(dtb[:, 0, :, :], tm[:, :, 0:NH], bc(pr[:, 0, :], 1, NT), ALU.add))
            V.scalar_tensor_tensor(dtb[:, 1, :, :], dtb[:, 0, :, :], -1.0, dtb[:, 0, :, :], ALU.mult, ALU.min).then_inc(dt_in, 1)
            V.tensor_scalar(dtb[:, 6, :, :], dtb[:, 0, :, :], 0.0, None, ALU.max)
            heads = lambda ap: ap.rearrange("p (h d) -> p h d", d=HD)
            dve.wait_ge(c_here, 16)
            for i in range(NT):
                for n in range(3):
                    await_taken(dve, "tm", n, i)
                q = heads(tm[:, i, TM_Q:TM_Q + D])
                at = C_ROPE + i * 4 * HD
                qc, qs = cst[:, at:at + HD], cst[:, at + HD:at + 2 * HD]
                if i:
                    dve.wait_ge(qr_ready, i)
                tt(qt[:, :, 0:HD // 2], q[:, :, HD // 2:HD], bc(qs[:, 0:HD // 2], 1, NH), ALU.mult)
                tt(qt[:, :, HD // 2:HD], q[:, :, 0:HD // 2], bc(qs[:, HD // 2:HD], 1, NH), ALU.mult)
                link(tt(qrs[i], q, bc(qc, 1, NH), ALU.mult))
                tt(qrs[i], qrs[i], qt, ALU.add).then_inc(qr_ready, 1)
            dve.wait_ge(dt_ln, 1)
            link(V.tensor_scalar(dtb[:, 4, :, :], dtb[:, 2, :, :], 1.0, None, ALU.add))
            link(V.tensor_scalar(dtb[:, 5, :, :], dtb[:, 4, :, :], -1.0, None, ALU.add))
            link(tt(dtb[:, 5, :, :], dtb[:, 2, :, :], dtb[:, 5, :, :], ALU.subtract))
            link(V.reciprocal(dtb[:, 4, :, :], dtb[:, 4, :, :]))
            link(tt(dtb[:, 5, :, :], dtb[:, 5, :, :], dtb[:, 4, :, :], ALU.mult))
            link(tt(dtb[:, 5, :, :], dtb[:, 5, :, :], dtb[:, 3, :, :], ALU.add))
            link(tt(dtb[:, 5, :, :], dtb[:, 5, :, :], dtb[:, 6, :, :], ALU.add))
            V.scalar_tensor_tensor(a_sb[:, :, :], dtb[:, 5, :, :], -1.0, bc(dtb[:, 7, 0, :], 1, NT), ALU.mult, ALU.mult).then_inc(a_ready, 1)
            dt = dtb[:, 5, :, :]
            dve.wait_ge(c_here, 16)
            await_taken(dve, "hidT", 1)
            dve.wait_ge(hTr_zero, 1)
            for g in range(GQ):
                last = V.tensor_copy(hTr[:, :, :, g, 0:NCMP], hTs[:, 1, :, :].rearrange("p c (k n) -> p c k n", k=NKV))
            last.then_inc(hTr_ready, 1)
            o = await_full(dve, "kc")[0:NCMP, 0:NKV * HD].rearrange("p (k d) -> p k d", k=NKV)
            cr = cst[0:NCMP, C_CROPE:C_CROPE + 2 * HD]
            link(tt(kcr, o, bc(cr[:, 0:HD], 1, NKV), ALU.mult))
            tt(kcr2[:, :, 0:HD // 2], o[:, :, HD // 2:HD], bc(cr[:, HD:HD + HD // 2], 1, NKV), ALU.mult)
            taken(tt(kcr2[:, :, HD // 2:HD], o[:, :, 0:HD // 2], bc(cr[:, HD + HD // 2:2 * HD], 1, NKV), ALU.mult), "kc")
            await_taken(dve, "kc")
            tt(kcr, kcr, kcr2, ALU.add).then_inc(kcr_ready, 1)
            o = await_full(dve, "vc")
            for kv in range(NKV):
                last = tt(Vbd[:, kv, :, :], bc(o[:, kv * HD:(kv + 1) * HD], 1, GQ), bc(cst[:, C_HEAD:C_HEAD + GQ], 2, HD), ALU.mult)
            taken(last, "vc")

            def rms(at, n, width, nth, value):
                dve.wait_ge(sq_ready, nth)
                V.tensor_scalar(st[:, at + 4:at + 4 + n], st[:, at:at + n], 1.0 / width, EPS, ALU.mult, ALU.add).then_inc(ms_ready, 1)
                dve.wait_ge(sd_ready, value)
                link(V.reciprocal(st[:, at:at + n], st[:, at + 8:at + 8 + n]))

            def statistics(src, at):
                for n in range(2):
                    last = V.bn_stats(bn[:, n, :], src[:, n * 512:(n + 1) * 512])
                link(last)
                link(V.bn_aggr(bna[:, :], bn[:, :, :]))
                V.tensor_scalar(st[:, at + 4:at + 5], bna[:, 1:2], EPS, None, ALU.add).then_inc(ms_ready, 1)

            def layer_norm(dst, src, scratch, which, at, value):
                dve.wait_ge(sd_ready, value)
                link(V.reciprocal(st[:, at:at + 1], st[:, at + 8:at + 9]))
                link(V.tensor_scalar(scratch, src, bna[:, 0:1], st[:, at:at + 1], ALU.subtract, ALU.mult))
                link(tt(scratch, scratch, lnw[:, 2 * which, :], ALU.mult))
                return tt(dst, scratch, lnw[:, 2 * which + 1, :], ALU.add)

            def ssd_gate(i):
                y = ymixes[i][:, 0:D]
                for n in range(2):
                    await_taken(dve, "z", n, i)
                tt(y, y, zs[:, i, :], ALU.mult).then_inc(y_ready, 1)

            def ssd_norm(i):
                y = ymixes[i][:, 0:D]
                dve.wait_ge(y_ready, i + 1)
                rms(0, NG, 512, i + 1, i + 1)
                for g in range(NG):
                    last = V.tensor_scalar(y[:, g * 512:(g + 1) * 512], y[:, g * 512:(g + 1) * 512], st[:, g:g + 1], None, ALU.mult)
                link(last)

            for i in range(NT):
                cols = slice(i * P, (i + 1) * P)
                dve.wait_ge(a_ready, 1)
                tt(Ma, bc(tri, 1, NH), bc(a_sb[:, i, :], 2, P), ALU.mult).then_inc(Ma_ready, 1)
                for half in range(2):
                    await_taken(dve, "xT", i, half)
                xi = heads(x_tm[:, i, :])
                tt(heads(xdt), xi, bc(dt[:, i, :], 2, HD), ALU.mult).then_inc(xdt_ready, 1)
                if i == 0:
                    dve.wait_ge(xdt_ready, 1)
                    await_taken(dve, "acs")
                    tt(heads(xdd), heads(xdt), bc(ea[:, 0, 1, :], 2, HD), ALU.mult).then_inc(xdd_ready, 1)
                o = await_full(dve, "cb", i)[:, 0:NG * P].rearrange("p (g l) -> p g l", g=NG)
                taken(tt(CBm[:, :, :], o, bc(tri, 1, NG), ALU.mult), "cb", i)
                await_taken(dve, "cb", i)
                for n in range(4):
                    await_taken(dve, "seg", i, n)
                    e4 = E[:, 4 * n:4 * n + 4, :]
                    tt(e4, e4, bc(CBm[:, n // 2, :], 1, 4), ALU.mult).then_inc(sco_ready, 1)
                y = ymixes[i][:, 0:D]
                link(tt(heads(y), xi, bc(pr[:, 2, :], 2, HD), ALU.mult))
                for g in range(NG):
                    yg = y[:, g * 512:(g + 1) * 512]
                    o = await_full(dve, "yd", i, g)
                    taken(tt(yg, yg, o, ALU.add), "yd", i, g)
                    await_taken(dve, "yd", i, g)
                    if i:
                        o = await_full(dve, "yo", g)
                        t = xdd[:, g * 512:(g + 1) * 512]
                        taken(tt(heads(t), heads(o), bc(ea[:, 1, 0, 8 * g:8 * g + 8], 2, HD), ALU.mult), "yo", g)
                        await_taken(dve, "yo", g)
                        link(tt(yg, yg, t, ALU.add))
                if i == NT - 1:
                    V.memset(st[:, 63:64], 0.0).then_inc(ssd_used, 1)

            def tail(i, part):
                if part == 0:
                    for n in range(4):
                        o = await_full(dve, "mT", i, n).rearrange("p (c t) -> p c t", c=4)
                        taken(tt(mixTs[i][:, 4 * n:4 * n + 4, :], o, bc(nw[:, 4 * n:4 * n + 4], 2, P), ALU.mult), "mT", i, n)
                elif part == 5:
                    dve.wait_ge(x_here, 16)
                    for n in range(2):
                        o = await_full(dve, "mix", i, n)
                        cols = slice(n * 512, (n + 1) * 512)
                        taken(V.scalar_tensor_tensor(r1s[i][:, cols], x_sb[:, i, cols], ALPHA, o, ALU.mult, ALU.add), "mix", i, n)
                    for n in range(2):
                        await_taken(dve, "mix", i, n)
                    statistics(r1s[i], 24)
                elif part == 6:
                    dve.wait_ge(ln_here, 64)
                    layer_norm(h_sb[:, i, :], r1s[i], junks[i], 0, 24, NT + 2 * i + 2).then_inc(h_ready, 1)
                elif part == 12:
                    for n in range(4):
                        o = await_full(dve, "qpT", i, n).rearrange("p (c t) -> p c t", c=4)
                        taken(V.tensor_copy(qpTs[i][:, 4 * n:4 * n + 4, :], o), "qpT", i, n)

            iota = cst[:, C_IOTA:C_IOTA + TOPK]

            def choose(u, par, part):
                count = [sum(CHOOSE_STEPS[:part])]

                def step(ins):
                    count[0] += 1
                    ins.then_inc(loop_step, 1)
                    await_alone(dve, dve_passed, loop_step, u * sum(CHOOSE_STEPS) + count[0])

                cells = lambda ap: ap.rearrange("p (a b) -> p a b", b=TOPK)
                if part <= 1:
                    c = part
                    if c == 0:
                        await_alone(dve, dve_passed, ks_ready, u + 1)
                    step(V.max(top[:, c, 0:8], ks[:, c, :]))
                    step(V.max_index(topi[:, c, 0:8], top[:, c, 0:8], ks[:, c, :]))
                    step(V.match_replace(ks2[:, c, :], top[:, c, 0:8], ks[:, c, :], BELOW))
                    step(V.max(top[:, c, 8:16], ks2[:, c, :]))
                    step(V.max_index(topi[:, c, 8:16], top[:, c, 8:16], ks2[:, c, :]))
                elif part == 2:
                    V.tensor_copy(topif, topi[:, :, :]).then_inc(ks_used, 1)
                    grid = cand.rearrange("p (a b) -> p a b", a=TOPK)
                    step(tt(grid, bc(top[:, 0, :], 2, TOPK), bc(top[:, 1, :], 1, TOPK), ALU.add))
                    step(V.max(gtop[:, 0:8], cand))
                    step(V.max_index(gpos[:, 0, 0:8], gtop[:, 0:8], cand))
                elif part == 3:
                    step(V.match_replace(cand2, gtop[:, 0:8], cand, BELOW))
                    step(V.max(gtop[:, 8:16], cand2))
                    V.tensor_scalar(gsm[:, 0:1], gtop[:, 0:1], -1.0, None, ALU.mult).then_inc(gs_ready, 1)
                    step(V.max_index(gpos[:, 0, 8:16], gtop[:, 8:16], cand2))
                elif part == 4:
                    V.tensor_scalar(gpos[:, 1, :], gpos[:, 0, :], 4, None, ALU.logical_shift_right)
                    step(V.tensor_scalar(gpos[:, 2, :], gpos[:, 0, :], TOPK - 1, None, ALU.bitwise_and))
                    step(V.tensor_copy(pij, gpos[:, 1:3, :]))
                    step(tt(cells(hot), bc(pij.rearrange("p c k -> p (c k)"), 2, TOPK), bc(iota, 1, 2 * TOPK), ALU.is_equal))
                elif part == 5:
                    for c in range(2):
                        half = slice(c * TOPK * TOPK, (c + 1) * TOPK * TOPK)
                        last = tt(cells(hot2[:, half]), cells(hot[:, half]), bc(topif[:, c, :], 1, TOPK), ALU.mult)
                    step(last)
                    step(V.tensor_reduce(eij.rearrange("p c k -> p (c k)"), cells(hot2), AX, ALU.add))
                    V.scalar_tensor_tensor(eidx[:, par, :], eij[:, 0, :], float(NKEY), eij[:, 1, :], ALU.mult, ALU.add).then_inc(idx_ready, 1)
                else:
                    dve.wait_ge(ge_ready, u + 1)
                    step(V.reciprocal(gsm[:, 2:3], gsm[:, 1:2]))
                    step(V.tensor_scalar(gate[:, par, :], gexp, gsm[:, 2:3], None, ALU.mult))
                assert count[0] == sum(CHOOSE_STEPS[:part + 1]), count

            def expert_start():
                await_taken(dve, "s", 0, 3)
                link(V.memset(zero, 0.0))
                link(V.memset(s_all[:, NT * PH * 2 * NKEY:], 0.0))
                V.memset(gsm[:, 2:3], 0.0).then_inc(zero_ready, 1)
                V.memset(gsm[:, 3:4], 0.0).then_inc(ks_used, 1)
                V.memset(gsm[:, 1:2], 0.0).then_inc(row_used, RING)

            def attention_norm(i):
                y = ymixes[i][:, D:2 * D]
                rms(12, 1, D, NT + i + 1, NT + 2 * i + 1)
                V.tensor_scalar(y, y, st[:, 12:13], None, ALU.mult).then_inc(ymix_ready, 1)

            for i in range(NT):
                o = await_full(dve, "sc", i)[:, 0:NH * NCMP].rearrange("p (h n) -> p h n", h=NH)
                bias = cst[:, C_CBIAS + i * NCMP:C_CBIAS + (i + 1) * NCMP]
                valid = cst[:, C_CVALID + i * NCMP:C_CVALID + (i + 1) * NCMP]
                taken(tt(Pe, o, bc(bias, 1, NH), ALU.add), "sc", i)
                await_taken(dve, "sc", i)
                link(V.tensor_reduce(cst1[:, 0, :], Pe, AX, ALU.max))
                tt(Pe, Pe, bc(cst1[:, 0, :], 2, NCMP), ALU.subtract).then_inc(cm_ready, 1)
                dve.wait_ge(ce_ready, i + 1)
                link(V.tensor_reduce(cst1[:, 1, :], Pe, AX, ALU.add))
                dve.wait_ge(sg_ready, 1)
                link(tt(Pe, Pe, bc(valid, 1, NH), ALU.mult))
                link(V.reciprocal(cst1[:, 2, :], cst1[:, 1, :]))
                gates = sg[:, i, :].rearrange("p (h b) -> p h b", b=3)
                link(tt(cst1[:, 3, :], cst1[:, 2, :], gates[:, :, 0], ALU.mult))
                dve.wait_ge(pc_zero, i + 1)
                tt(Pc[:, :, 0:NCMP], Pe, bc(cst1[:, 3, :], 2, NCMP), ALU.mult).then_inc(pc_ready, 1)
                if i:
                    attention_norm(i - 1)

                def maxima(u):
                    o = await_full(dve, "S", i, u)
                    V.tensor_reduce(nmx[:, u, :], o.rearrange("p (e t) -> p e t", e=2)[:, :, 0:(i + 1) * P], AX, ALU.max, negate=True).then_inc(nm_ready, 1)

                ahead = AHEAD[i]
                for u in range(-ahead, len(UN)):
                    if u >= 0:
                        kv, gp, b = UN[u]
                        h = kv * GQ + 2 * gp
                        await_taken(dve, "S", i, u)
                        link(V.reciprocal(coef[:, u, :], lsum[:, u, :]))
                        link(tt(coef[:, u, :], coef[:, u, :], gates[:, h:h + 2, 1 + b], ALU.mult))
                        for e in range(2):
                            part = Pb[:, u % (ahead + 1), e, 0:(i + 1) * P]
                            last = V.tensor_scalar(part, part, coef[:, u, e:e + 1], None, ALU.mult)
                        last.then_inc(p_ready, 1)
                    if u + ahead < len(UN):
                        maxima(u + ahead)
                    if i == 0 and u in GATE_AT:
                        ssd_gate(GATE_AT.index(u))
                    if i == 0 and u - 1 in GATE_AT:
                        ssd_norm(GATE_AT.index(u - 1))
                    if i == 1 and u >= 0:
                        for part in TAIL_AT[u]:
                            tail(0, part)
                        for part in CHOICE_AT[u]:
                            if part == 0:
                                expert_start()
                            choose(0, 0, part)
                dve.wait_ge(pv_done, len(UN) * (i + 1))
                y = ymixes[i][:, D:2 * D]
                for n in range(2):
                    V.tensor_copy(y[:, n * 512:(n + 1) * 512], ps[:, 6 + n, :]).then_inc(o_taken, 1)
                if i == NT - 1:
                    attention_norm(i)



            def weigh(u, e, k):
                dve.wait_ge(w_step, u * TOPK + (k + 1))
                dve.wait_ge(row_used, u * TOPK + (k + 1 + RING - DIAGS))
                V.tensor_scalar(diag[:, k % DIAGS, :], ident, wact[:, e, 0, k:k + 1], gate[:, e, k:k + 1], ALU.mult, ALU.mult).then_inc(diag_ready, 1)

            def head(i, u, pair, e):
                weighed = 0
                for k in range(TOPK):
                    n = e * TOPK + k
                    slot = place(i, pair * 2 * TOPK + n if i == 0 else n)
                    dve.wait_ge(row_here[slot], 16 * arrivals(i, pair, n))
                    if not (isinstance(u, int) and u + k == 0):
                        dve.wait_ge(dot_done, u * TOPK + k)
                    V.tensor_tensor_reduce(out=dotj, in0=row(slot)[:, 0:D], in1=h_sb[:, i, :], scale=1.0, scalar=0.0,
                                           op0=ALU.mult, op1=ALU.add, accum_out=hdot[:, e, k:k + 1]).then_inc(dot_done, 1)
                    part = (u * TOPK + k) // PART_EVERY if i == 0 and (k + 1) % PART_EVERY == 0 else PARTS
                    upto = k + 1 if part < PARTS or k == TOPK - 1 else max(weighed, k + 1 - LAG)
                    for j in range(weighed, upto):
                        weigh(u, e, j)
                    weighed = upto
                    if CHOOSE_AT <= k < CHOOSE_AT + len(CHOOSE_STEPS):
                        choose(u + 1, 1 - e, k - CHOOSE_AT)
                    if part < PARTS:
                        tail(1, part)

            def finish(i):
                for n in range(2):
                    o = await_full(dve, "y", i, n)
                    part = slice(n * 512, (n + 1) * 512)
                    taken(V.scalar_tensor_tensor(acc2[:, part], h_sb[:, i, part], ALPHA, o, ALU.mult, ALU.add), "y", i, n)
                for n in range(2):
                    await_taken(dve, "y", i, n)
                statistics(acc2, 36)
                layer_norm(outb[i], acc2, acc2, 1, 36, 3 * NT + i + 1).then_inc(out_ready, 1)

            for u in range(PH):
                head(0, u, u // 2, u % 2)
            finish(0)
            with dve.Fori(0, PH // 2) as pair:
                for e in range(2):
                    head(1, pair * 2 + (PH + e), pair, e)
            finish(1)

        @block.gpsimd
        def _(pool):
            G = nc.gpsimd
            steps = [0]

            def link(ins):
                steps[0] += 1
                ins.then_inc(pool_step, 1)
                pool.wait_ge(pool_step, steps[0])

            G.memset(xbcT[:, :, 0:TAPS - 1], 0.0).then_inc(pads_zero, 1)
            G.memset(hTr.rearrange("p c k g n -> p (c k g n)"), 0.0).then_inc(hTr_zero, 1)
            pool.wait_ge(prm_here, 80)
            for c in range(2, 4):
                await_taken(pool, "cmp", c)
            add_position(G, 1).then_inc(X_ready[1], 1)
            pool.wait_ge(c_here, 16)
            for i in range(NT):
                for n in range(3, len(TM_PIECES)):
                    await_taken(pool, "tm", n, i)
                if i:
                    for b in range(2):
                        await_full(pool, "kT", i - 1, b)
                else:
                    for w in range(2):
                        await_full(pool, "hid", w)
                at = C_ROPE + i * 4 * HD + 2 * HD
                kc, ksin = cst[:, at:at + HD], cst[:, at + HD:at + 2 * HD]
                for b, dst in enumerate((kr, kr2)):
                    src = tm[:, i, TM_KV + 512 * b:TM_KV + 512 * b + NKV * HD].rearrange("p (h d) -> p h d", d=HD)
                    G.tensor_tensor(krt[:, :, 0:HD // 2], src[:, :, HD // 2:HD], bc(ksin[:, 0:HD // 2], 1, NKV), ALU.mult)
                    G.tensor_tensor(krt[:, :, HD // 2:HD], src[:, :, 0:HD // 2], bc(ksin[:, HD // 2:HD], 1, NKV), ALU.mult)
                    link(G.tensor_tensor(dst, src, bc(kc, 1, NKV), ALU.mult))
                    G.tensor_tensor(dst, dst, krt, ALU.add).then_inc(kr_ready, 1)
                    pool.wait_ge(kr_ready, 2 * i + b + 1)
                if i:
                    await_full(pool, "pcT", i - 1)
                else:
                    pool.wait_ge(ssd_used, 1)
                G.memset(Pc.rearrange("p h n -> p (h n)"), 0.0).then_inc(pc_zero, 1)

            def gathers(i, u, pair, e):
                pool.wait_ge(idx_ready, u + 1)
                for k in range(TOPK):
                    n = e * TOPK + k
                    slot = place(i, pair * 2 * TOPK + n if i == 0 else n)
                    if i or u * TOPK + k >= RING0:
                        await_alone(pool, pool_passed, row_used, u * TOPK + (k + 1 + (RING - RING0 if i == 0 else 0)))
                    G.indirect_dma_start(row(slot), None, uv, bass.IndirectOffsetOnAxis(eidx[:, e, k:k + 1], 0)).then_inc(row_here[slot], 16)

            for u in range(PH):
                gathers(0, u, u // 2, u % 2)
            await_full(pool, "q", NT - 1, 3)
            with pool.Fori(0, PH // 2) as pair:
                for e in range(2):
                    gathers(1, pair * 2 + (PH + e), pair, e)


_INPUTS = ["x", "xT", "w_in", "conv", "prm", "normw", "posT", "w1", "w2", "w_out", "ln", "wq", "skT", "uv", "const"]


def arrange(x, w_in, conv_w, conv_b, dt_bias, a_log, d_skip, ssd_norm_w, cmp_pos_k, cmp_w1_k, cmp_w2_k,
            cmp_pos_v, cmp_w1_v, cmp_w2_v, attn_norm_w, w_out, ln1_g, ln1_b, peer_w_query, peer_sub_keys,
            peer_u, peer_v, ln2_g, ln2_b):
    a = lambda v: np.asarray(v)[0]
    return {
        "x": a(x), "xT": a(x).T, "w_in": a(w_in),
        "conv": np.concatenate([a(conv_w), a(conv_b)[None]]).reshape(TAPS + 1, NCONV, P).transpose(2, 1, 0),
        "prm": np.concatenate([a(dt_bias), a(a_log), a(d_skip)])[None],
        "normw": np.concatenate([a(ssd_norm_w), a(attn_norm_w)]).reshape(2 * KD, P).T,
        "posT": np.stack([a(cmp_pos_k), a(cmp_pos_v)]).reshape(2, CLEN // 2, P).transpose(2, 0, 1),
        "w1": np.stack([a(cmp_w1_k), a(cmp_w1_v)]), "w2": np.stack([a(cmp_w2_k), a(cmp_w2_v)]),
        "w_out": a(w_out), "ln": np.stack([a(ln1_g), a(ln1_b), a(ln2_g), a(ln2_b)]), "wq": a(peer_w_query),
        "skT": a(peer_sub_keys).reshape(2 * PH, NKEY, P).transpose(2, 0, 1),
        "uv": np.concatenate([a(peer_u), a(peer_v)], axis=1), "const": constants(),
    }


def kernel(**inputs):
    import concourse.bacc as bacc
    from concourse.bass_utils import run_bass_kernel_spmd

    nc = bacc.Bacc("TRN2", target_bir_lowering=False, num_devices=1)
    arrays = {f"in_{n}": np.ascontiguousarray(v) for n, v in arrange(**inputs).items()}
    args = [nc.dram_tensor(f"in_{n}", arrays[f"in_{n}"].shape, mybir.dt.float32, kind="ExternalInput").ap() for n in _INPUTS]
    out = nc.dram_tensor("out", (T, D), mybir.dt.float32, kind="ExternalOutput").ap()
    layer(nc, *args, out)
    r = run_bass_kernel_spmd(nc, [arrays], core_ids=[0])
    return r.results[0]["out"].reshape(1, T, D)
```
